# Optimizing a Trainium2 kernel written in Bass

```python
import jax
import jax.numpy as jnp
from jax import lax
import numpy as np

D_MODEL = 1024
BATCH = 1
SEQ = 512
DEPTH = 2

GRID_W = 64
CTX_LEN = 256
ROPE_THETA = 10000.0
RMS_EPS = 1e-6

GLA_HEADS = 4
GLA_DK = 64
GLA_DV = 128
GLA_RANK = 16
GLA_TAU = 16.0
GLA_CHUNK = 64

SWA_HEADS = 8
SWA_KV_HEADS = 2
SWA_HD = 64
WINDOW = 128
SWA_BLOCK = WINDOW

MLA_HEADS = 8
MLA_Q_RANK = 512
MLA_KV_RANK = 256
MLA_NOPE = 128
MLA_ROPE = 64
MLA_V = 128
MLA_BLOCK = 128
MLA_SCALE = (MLA_NOPE + MLA_ROPE) ** -0.5

N_EXPERTS = 64
TOP_K = 8
N_GROUPS = 8
TOPK_GROUPS = 4
D_EXPERT = 256
D_SHARED = 256
ROUTED_SCALE = 2.5
MOE_BLOCK = 128

EVEN_SPLITS = (GLA_HEADS * GLA_DK, GLA_HEADS * GLA_DK, GLA_HEADS * GLA_DV, GLA_HEADS * GLA_DV, GLA_RANK, GLA_RANK, SWA_HEADS * SWA_HD, SWA_KV_HEADS * SWA_HD, SWA_KV_HEADS * SWA_HD)
EVEN_IN = sum(EVEN_SPLITS)
EVEN_OUT = GLA_HEADS * GLA_DV + SWA_HEADS * SWA_HD
ODD_SPLITS = (MLA_Q_RANK, MLA_KV_RANK, MLA_ROPE)
ODD_IN = sum(ODD_SPLITS)
ODD_OUT = MLA_HEADS * MLA_V
N_EVEN = (DEPTH + 1) // 2
N_ODD = DEPTH // 2

kernel_name = "hybrid_gla_swa_mla_moe_dit"

def rmsnorm(x, g):
    xf = x.astype(jnp.float32)
    y = xf * lax.rsqrt(jnp.mean(xf * xf, axis=-1, keepdims=True) + RMS_EPS)
    return y.astype(x.dtype) * g

def modulate(x, g, shift, scale):
    return rmsnorm(x, g) * (1 + scale) + shift

def split_cols(z, sizes):
    cuts = [int(s) for s in np.cumsum(sizes)[:-1]]
    return jnp.split(z, cuts, axis=-1)

def axial_rope_angles(seq_len, rot_dim):
    rows = seq_len // GRID_W
    row = jnp.repeat(jnp.arange(rows, dtype=jnp.float32), GRID_W)
    col = jnp.tile(jnp.arange(GRID_W, dtype=jnp.float32), rows)
    axis_dim = rot_dim // 2
    inv_freq = ROPE_THETA ** (-jnp.arange(0, axis_dim, 2, dtype=jnp.float32) / axis_dim)
    return jnp.concatenate([row[:, None] * inv_freq, col[:, None] * inv_freq], axis=-1)

def apply_rope(x, ang):
    seq_len, half = ang.shape
    a = ang.reshape((1, seq_len) + (1,) * (x.ndim - 3) + (half,))
    cos, sin = jnp.cos(a), jnp.sin(a)
    xf = x.astype(jnp.float32)
    x1, x2 = xf[..., :half], xf[..., half:]
    return jnp.concatenate([x1 * cos - x2 * sin, x2 * cos + x1 * sin], axis=-1).astype(x.dtype)

def gla_log_decay(a_low, wa2, ba):
    return jax.nn.log_sigmoid((a_low @ wa2 + ba).astype(jnp.float32)) / GLA_TAU

def gla_chunk_scan(q, k, v, log_a, s0):
    b_, length, h, _ = q.shape
    dv = v.shape[-1]
    n = length // GLA_CHUNK

    def to_chunks(t):
        return t.astype(jnp.float32).reshape(b_, n, GLA_CHUNK, h, t.shape[-1]).transpose(1, 0, 3, 2, 4)

    incl = jnp.tril(jnp.ones((GLA_CHUNK, GLA_CHUNK), dtype=bool))[None, None, :, :, None]

    def step(state, inp):
        qc, kc, vc, ac = inp
        cum = jnp.cumsum(ac, axis=2)
        o = jnp.einsum('bhcd,bhde->bhce', qc * jnp.exp(cum), state)
        rel = jnp.exp(jnp.where(incl, cum[:, :, :, None, :] - cum[:, :, None, :, :], -jnp.inf))
        scores = jnp.einsum('bhijd,bhjd->bhij', qc[:, :, :, None, :] * rel, kc)
        o = o + jnp.einsum('bhij,bhje->bhie', scores, vc)
        last = cum[:, :, -1:, :]
        state = jnp.exp(last[:, :, 0, :])[..., None] * state + jnp.einsum('bhjd,bhje->bhde', kc * jnp.exp(last - cum), vc)
        return state, o

    s_fin, o = lax.scan(step, s0, (to_chunks(q), to_chunks(k), to_chunks(v), to_chunks(log_a)))
    o = o.transpose(1, 0, 3, 2, 4).reshape(b_, length, h, dv)
    return o.astype(v.dtype), s_fin

def gla_bidir(q, k, v, la_f, la_b, s_f, s_b):
    o_f, s_f = gla_chunk_scan(q, k, v, la_f, s_f)
    flip = lambda t: jnp.flip(t, axis=1)
    o_b, s_b = gla_chunk_scan(flip(q), flip(k), flip(v), flip(la_b), s_b)
    return o_f + flip(o_b), s_f, s_b

def gla_output(o, g, norm_g):
    b_, length = g.shape[:2]
    return rmsnorm(o, norm_g).reshape(b_, length, -1) * jax.nn.silu(g)

def swa_context(q, k, v, sink):
    b_, length = q.shape[:2]
    g = SWA_HEADS // SWA_KV_HEADS
    qg = q.reshape(b_, length, SWA_KV_HEADS, g, SWA_HD)
    s = jnp.einsum('bqhgd,bkhd->bhgqk', qg, k).astype(jnp.float32) * (SWA_HD ** -0.5)
    sink_b = jnp.broadcast_to(sink.reshape(1, SWA_KV_HEADS, g, 1, 1).astype(jnp.float32), s.shape[:-1] + (1,))
    p = jax.nn.softmax(jnp.concatenate([sink_b, s], axis=-1), axis=-1)[..., 1:].astype(v.dtype)
    o = jnp.einsum('bhgqk,bkhd->bqhgd', p, v)
    return o.reshape(b_, length, SWA_HEADS * SWA_HD)

def swa_latent(q, k, v, k_ctx, v_ctx, sink):
    b_, length = q.shape[:2]
    g = SWA_HEADS // SWA_KV_HEADS
    blk = SWA_BLOCK
    nb = length // blk
    scale = SWA_HD ** -0.5
    qb = q.reshape(b_, nb, blk, SWA_KV_HEADS, g, SWA_HD)

    def band(t):
        tp = jnp.pad(t, ((0, 0), (blk, blk), (0, 0), (0, 0))).reshape(b_, nb + 2, blk, SWA_KV_HEADS, SWA_HD)
        return jnp.concatenate([tp[:, :-2], tp[:, 1:-1], tp[:, 2:]], axis=2)

    kw, vw = band(k), band(v)
    s_win = jnp.einsum('bnqhgd,bnshd->bnhgqs', qb, kw).astype(jnp.float32) * scale
    s_ctx = jnp.einsum('bnqhgd,bchd->bnhgqc', qb, k_ctx).astype(jnp.float32) * scale
    qi = jnp.arange(blk)[:, None]
    si = jnp.arange(3 * blk)[None, :]
    kpos = jnp.arange(nb)[:, None, None] * blk - blk + si[None]
    valid = (jnp.abs(si - blk - qi) <= WINDOW)[None] & (kpos >= 0) & (kpos < length)
    s_win = jnp.where(valid[None, :, None, None], s_win, -jnp.inf)
    sink_b = jnp.broadcast_to(sink.reshape(1, 1, SWA_KV_HEADS, g, 1, 1).astype(jnp.float32), s_win.shape[:-1] + (1,))
    p = jax.nn.softmax(jnp.concatenate([sink_b, s_ctx, s_win], axis=-1), axis=-1).astype(v.dtype)
    n_ctx = k_ctx.shape[1]
    o = (jnp.einsum('bnhgqc,bchd->bnqhgd', p[..., 1:1 + n_ctx], v_ctx)
         + jnp.einsum('bnhgqs,bnshd->bnqhgd', p[..., 1 + n_ctx:], vw))
    return o.reshape(b_, length, SWA_HEADS * SWA_HD)

def even_project(u, w_in, wa2, ba):
    b_, length = u.shape[:2]
    q, k, v, g, a_f, a_b, sq, sk, sv = split_cols(u @ w_in, EVEN_SPLITS)
    heads = lambda t, h: t.reshape(b_, length, h, -1)
    la_f = gla_log_decay(a_f, wa2[0], ba[0])
    la_b = gla_log_decay(a_b, wa2[1], ba[1])
    return (heads(q * GLA_DK ** -0.5, GLA_HEADS), heads(k, GLA_HEADS), heads(v, GLA_HEADS), g,
            heads(la_f, GLA_HEADS), heads(la_b, GLA_HEADS),
            heads(sq, SWA_HEADS), heads(sk, SWA_KV_HEADS), heads(sv, SWA_KV_HEADS))

def even_mixer(ul, uc, w_in, wa2, ba, norm_g, sink, w_out, ang, need_ctx):
    cq, ck, cv, cg, claf, clab, csq, csk, csv = even_project(uc, w_in, wa2, ba)
    lq, lk, lv, lg, llaf, llab, lsq, lsk, lsv = even_project(ul, w_in, wa2, ba)
    zero = jnp.zeros((uc.shape[0], GLA_HEADS, GLA_DK, GLA_DV), jnp.float32)
    o_c, s_f, s_b = gla_bidir(cq, ck, cv, claf, clab, zero, zero)
    o_l, _, _ = gla_bidir(lq, lk, lv, llaf, llab, s_f, s_b)
    a_l = swa_latent(apply_rope(lsq, ang), apply_rope(lsk, ang), lsv, csk, csv, sink)
    y_l = jnp.concatenate([gla_output(o_l, lg, norm_g), a_l], axis=-1) @ w_out
    y_c = None
    if need_ctx:
        a_c = swa_context(csq, csk, csv, sink)
        y_c = jnp.concatenate([gla_output(o_c, cg, norm_g), a_c], axis=-1) @ w_out
    return y_l, y_c

def mla_project(u, w_in, q_norm, kv_norm, w_uq, w_ukv):
    b_, length = u.shape[:2]
    cq, ckv, k_rope = split_cols(u @ w_in, ODD_SPLITS)
    q = (rmsnorm(cq, q_norm) @ w_uq).reshape(b_, length, MLA_HEADS, MLA_NOPE + MLA_ROPE)
    kv = (rmsnorm(ckv, kv_norm) @ w_ukv).reshape(b_, length, MLA_HEADS, MLA_NOPE + MLA_V)
    return q[..., :MLA_NOPE], q[..., MLA_NOPE:], kv[..., :MLA_NOPE], kv[..., MLA_NOPE:], k_rope

def mla_scores(qn, qr, kn, kr):
    s = jnp.einsum('bqhd,bkhd->bhqk', qn, kn) + jnp.einsum('bqhr,bkr->bhqk', qr, kr)
    return s.astype(jnp.float32) * MLA_SCALE

def mla_context(qn, qr, kn, kr, v):
    p = jax.nn.softmax(mla_scores(qn, qr, kn, kr), axis=-1).astype(v.dtype)
    return jnp.einsum('bhqk,bkhd->bqhd', p, v)

def mla_latent(qn, qr, kn, kr, v, kn_c, kr_c, v_c):
    b_, length = qn.shape[:2]
    nb = length // MLA_BLOCK
    n_ctx = kn_c.shape[1]

    def blocks(t):
        return t.reshape((b_, nb, MLA_BLOCK) + t.shape[2:]).swapaxes(0, 1)

    def attend(args):
        qn_i, qr_i = args
        s = jnp.concatenate([mla_scores(qn_i, qr_i, kn_c, kr_c), mla_scores(qn_i, qr_i, kn, kr)], axis=-1)
        p = jax.nn.softmax(s, axis=-1).astype(v.dtype)
        return (jnp.einsum('bhqc,bchd->bqhd', p[..., :n_ctx], v_c)
                + jnp.einsum('bhqk,bkhd->bqhd', p[..., n_ctx:], v))

    o = lax.map(attend, (blocks(qn), blocks(qr)))
    return o.swapaxes(0, 1).reshape(b_, length, MLA_HEADS * MLA_V)

def odd_mixer(ul, uc, w_in, q_norm, kv_norm, w_uq, w_ukv, w_out, ang, need_ctx):
    b_, length = ul.shape[:2]
    lqn, lqr, lkn, lv, lkr = mla_project(ul, w_in, q_norm, kv_norm, w_uq, w_ukv)
    cqn, cqr, ckn, cv, ckr = mla_project(uc, w_in, q_norm, kv_norm, w_uq, w_ukv)
    o_l = mla_latent(lqn, apply_rope(lqr, ang), lkn, apply_rope(lkr, ang), lv, ckn, ckr, cv)
    y_l = o_l @ w_out
    y_c = None
    if need_ctx:
        y_c = mla_context(cqn, cqr, ckn, ckr, cv).reshape(uc.shape[0], uc.shape[1], -1) @ w_out
    return y_l, y_c

def route(h, w_router, b_corr):
    t = h.shape[0]
    scores = jax.nn.sigmoid(h.astype(jnp.float32) @ w_router.astype(jnp.float32))
    sel = scores + b_corr.astype(jnp.float32)
    grp = lax.top_k(sel.reshape(t, N_GROUPS, N_EXPERTS // N_GROUPS), 2)[0].sum(-1)
    _, gidx = lax.top_k(grp, TOPK_GROUPS)
    gmask = jax.nn.one_hot(gidx, N_GROUPS, dtype=jnp.float32).sum(1)
    emask = jnp.repeat(gmask, N_EXPERTS // N_GROUPS, axis=1) > 0
    _, idx = lax.top_k(jnp.where(emask, sel, -jnp.inf), TOP_K)
    w = jnp.take_along_axis(scores, idx, axis=1)
    w = w / jnp.sum(w, axis=-1, keepdims=True) * ROUTED_SCALE
    return idx, w

def moe(h, w_router, b_corr, w_g, w_u, w_d, ws_g, ws_u, ws_d):
    t, d = h.shape
    idx, wts = route(h, w_router, b_corr)
    n_assign = t * TOP_K
    flat_e = idx.reshape(-1)
    flat_t = jnp.repeat(jnp.arange(t, dtype=jnp.int32), TOP_K)
    flat_w = wts.reshape(-1)
    order = jnp.argsort(flat_e)
    se, st, sw = flat_e[order], flat_t[order], flat_w[order]
    counts = jnp.bincount(flat_e, length=N_EXPERTS)
    starts = jnp.cumsum(counts) - counts
    padded = (counts + MOE_BLOCK - 1) // MOE_BLOCK * MOE_BLOCK
    pad_end = jnp.cumsum(padded)
    pad_start = pad_end - padded
    dest = pad_start[se] + (jnp.arange(n_assign) - starts[se])
    n_blk = -(-n_assign // MOE_BLOCK) + N_EXPERTS
    buf_tok = jnp.zeros((n_blk * MOE_BLOCK,), jnp.int32).at[dest].set(st)
    buf_w = jnp.zeros((n_blk * MOE_BLOCK,), jnp.float32).at[dest].set(sw)
    blk_start = jnp.arange(n_blk, dtype=pad_end.dtype) * MOE_BLOCK
    blk_e = jnp.minimum(jnp.searchsorted(pad_end, blk_start, side='right'), N_EXPERTS - 1)

    def expert_block(args):
        tok, wt, e = args
        xb = h[tok]
        hid = jax.nn.silu(xb @ w_g[e]) * (xb @ w_u[e])
        return (hid @ w_d[e]) * wt[:, None].astype(h.dtype)

    yb = lax.map(expert_block, (buf_tok.reshape(n_blk, MOE_BLOCK), buf_w.reshape(n_blk, MOE_BLOCK), blk_e))
    routed = jnp.zeros_like(h).at[buf_tok].add(yb.reshape(-1, d))
    shared = (jax.nn.silu(h @ ws_g) * (h @ ws_u)) @ ws_d
    return shared + routed

def setup_inputs(seed: int = 0) -> dict:
    key = jax.random.key(seed)
    ks = jax.random.split(key, 30)
    d = D_MODEL

    def nrm(i, shape, scale):
        return jax.random.normal(ks[i], shape, jnp.float32) * scale

    return {
        'x': nrm(0, (BATCH, SEQ, d), 1.0),
        'c': nrm(1, (BATCH, d), 1.0),
        'ctx': nrm(2, (BATCH, CTX_LEN, d), 1.0),
        'c_ctx': nrm(3, (d,), 1.0),
        'w_mod': nrm(4, (DEPTH, d, 6 * d), 0.5 * d ** -0.5),
        'b_mod': nrm(5, (DEPTH, 6 * d), 0.02),
        'g_mix_pre': 1.0 + nrm(6, (DEPTH, d), 0.05),
        'g_mix_post': 1.0 + nrm(7, (DEPTH, d), 0.05),
        'g_ffn_pre': 1.0 + nrm(8, (DEPTH, d), 0.05),
        'g_ffn_post': 1.0 + nrm(9, (DEPTH, d), 0.05),
        'w_in_e': nrm(10, (N_EVEN, d, EVEN_IN), d ** -0.5),
        'gla_wa2': nrm(11, (N_EVEN, 2, GLA_RANK, GLA_HEADS * GLA_DK), GLA_RANK ** -0.5),
        'gla_ba': nrm(12, (N_EVEN, 2, GLA_HEADS * GLA_DK), 0.5),
        'gla_norm': 1.0 + nrm(13, (N_EVEN, GLA_DV), 0.05),
        'swa_sink': nrm(14, (N_EVEN, SWA_HEADS), 0.5),
        'w_out_e': nrm(15, (N_EVEN, EVEN_OUT, d), EVEN_OUT ** -0.5),
        'w_in_o': nrm(16, (N_ODD, d, ODD_IN), d ** -0.5),
        'mla_q_norm': 1.0 + nrm(17, (N_ODD, MLA_Q_RANK), 0.05),
        'mla_kv_norm': 1.0 + nrm(18, (N_ODD, MLA_KV_RANK), 0.05),
        'w_uq': nrm(19, (N_ODD, MLA_Q_RANK, MLA_HEADS * (MLA_NOPE + MLA_ROPE)), MLA_Q_RANK ** -0.5),
        'w_ukv': nrm(20, (N_ODD, MLA_KV_RANK, MLA_HEADS * (MLA_NOPE + MLA_V)), MLA_KV_RANK ** -0.5),
        'w_out_o': nrm(21, (N_ODD, ODD_OUT, d), ODD_OUT ** -0.5),
        'w_router': nrm(22, (DEPTH, d, N_EXPERTS), d ** -0.5),
        'b_router': nrm(23, (DEPTH, N_EXPERTS), 0.01),
        'w_exp_gate': nrm(24, (DEPTH, N_EXPERTS, d, D_EXPERT), d ** -0.5),
        'w_exp_up': nrm(25, (DEPTH, N_EXPERTS, d, D_EXPERT), d ** -0.5),
        'w_exp_down': nrm(26, (DEPTH, N_EXPERTS, D_EXPERT, d), D_EXPERT ** -0.5),
        'w_sh_gate': nrm(27, (DEPTH, d, D_SHARED), d ** -0.5),
        'w_sh_up': nrm(28, (DEPTH, d, D_SHARED), d ** -0.5),
        'w_sh_down': nrm(29, (DEPTH, D_SHARED, d), D_SHARED ** -0.5),
    }

def reference(x, c, ctx, c_ctx, w_mod, b_mod, g_mix_pre, g_mix_post, g_ffn_pre, g_ffn_post,
              w_in_e, gla_wa2, gla_ba, gla_norm, swa_sink, w_out_e,
              w_in_o, mla_q_norm, mla_kv_norm, w_uq, w_ukv, w_out_o,
              w_router, b_router, w_exp_gate, w_exp_up, w_exp_down, w_sh_gate, w_sh_up, w_sh_down):
    b_, seq_len, d = x.shape
    ang_swa = axial_rope_angles(seq_len, SWA_HD)
    ang_mla = axial_rope_angles(seq_len, MLA_ROPE)
    hl, hc = x, ctx
    for l in range(DEPTH):
        last = l == DEPTH - 1
        mod_l = (jax.nn.silu(c) @ w_mod[l] + b_mod[l])[:, None, :]
        mod_c = (jax.nn.silu(c_ctx) @ w_mod[l] + b_mod[l])[None, None, :]
        sh_a, sc_a, gt_a, sh_f, sc_f, gt_f = jnp.split(mod_l, 6, axis=-1)
        csh_a, csc_a, cgt_a, csh_f, csc_f, cgt_f = jnp.split(mod_c, 6, axis=-1)
        ul = modulate(hl, g_mix_pre[l], sh_a, sc_a)
        uc = modulate(hc, g_mix_pre[l], csh_a, csc_a)
        i = l // 2
        if l % 2 == 0:
            yl, yc = even_mixer(ul, uc, w_in_e[i], gla_wa2[i], gla_ba[i], gla_norm[i], swa_sink[i], w_out_e[i], ang_swa, not last)
        else:
            yl, yc = odd_mixer(ul, uc, w_in_o[i], mla_q_norm[i], mla_kv_norm[i], w_uq[i], w_ukv[i], w_out_o[i], ang_mla, not last)
        hl = hl + gt_a * rmsnorm(yl, g_mix_post[l])
        vl = modulate(hl, g_ffn_pre[l], sh_f, sc_f)
        moe_w = (w_router[l], b_router[l], w_exp_gate[l], w_exp_up[l], w_exp_down[l], w_sh_gate[l], w_sh_up[l], w_sh_down[l])
        if last:
            fl = moe(vl.reshape(-1, d), *moe_w).reshape(b_, seq_len, d)
        else:
            hc = hc + cgt_a * rmsnorm(yc, g_mix_post[l])
            vc = modulate(hc, g_ffn_pre[l], csh_f, csc_f)
            n_c = vc.shape[0] * vc.shape[1]
            f = moe(jnp.concatenate([vc.reshape(-1, d), vl.reshape(-1, d)], axis=0), *moe_w)
            hc = hc + cgt_f * rmsnorm(f[:n_c].reshape(hc.shape), g_ffn_post[l])
            fl = f[n_c:].reshape(b_, seq_len, d)
        hl = hl + gt_f * rmsnorm(fl, g_ffn_post[l])
    return hl


_drawn_inputs = setup_inputs


def setup_inputs(seed=0):
    import zlib

    import numpy as np

    out = dict(_drawn_inputs(seed))
    spreads = {}
    factors = {'swa_sink': 8.0, 'mla_q_norm': 4.637}
    for name, (base, spread) in spreads.items():
        noise = np.random.default_rng([zlib.crc32(name.encode()), seed]).standard_normal(out[name].shape)
        drawn = base * np.exp(spread * noise) if base else spread * noise
        out[name] = jnp.asarray(drawn.astype(out[name].dtype))
    for name, factor in factors.items():
        out[name] = (out[name] * factor).astype(out[name].dtype)
    return out
```

```python
from contextlib import ExitStack

import numpy as np

import concourse.bass as bass
from concourse import mybir

F32 = mybir.dt.float32
I32 = mybir.dt.int32
ALU = mybir.AluOpType
ACT = mybir.ActivationFunctionType
AX = mybir.AxisListType.X

P = 128
D = 1024
KD = D // P
NCTX, NLAT = 256, 512
T = NCTX + NLAT
NT = T // P
CT = NCTX // P
DEPTH = 2
EPS = 1e-6

GH, GDK, GDV, GRANK, GTAU = 4, 64, 128, 16, 16.0
SH, SKV, SHD, WIN = 8, 2, 64, 128
MH, MQR, MKR, MN, MR, MV = 8, 512, 256, 128, 64, 128
MSCALE = float((MN + MR) ** -0.5)
NE, TOPK, NG, TG, DE = 64, 8, 8, 4, 256
EG = NE // NG
ROUTED = 2.5
NEG = -1.0e30

Q0 = 0
K0 = Q0 + GH * GDK
V0 = K0 + GH * GDK
G0 = V0 + GH * GDV
A0 = G0 + GH * GDV
SQ0 = A0 + 2 * GRANK
SK0 = SQ0 + SH * SHD
SV0 = SK0 + SKV * SHD
EVEN_IN = SV0 + SKV * SHD
ODD_IN = MQR + MKR + MR

MAXBLK = T * TOPK // P + NE
SLOTB = 128
QUADS = 4
LOADED = 4


def bcast(col, n):
    return col.to_broadcast([col.shape[0], n])


class Trunk:

    def __init__(self, nc, dram, out):
        self.nc, self.dram, self.out = nc, dram, out


class Phase:

    opened = 0

    def __init__(self, nc):
        self.nc = nc

    def __enter__(self):
        Phase.opened += 1
        self.tag = f"p{Phase.opened}_"
        self.stack = ExitStack()
        self.stack.__enter__()
        self.sems = []
        return self

    def sb(self, name, shape, dt=F32):
        return self.stack.enter_context(self.nc.sbuf_tensor(self.tag + name, shape, dt))

    def ps(self, name, shape, dt=F32):
        return self.stack.enter_context(self.nc.psum_tensor(self.tag + name, shape, dt))

    def sem(self, name):
        s = self.nc.alloc_semaphore(self.tag + name)
        self.sems.append(s)
        return s

    def adopt(self, sems):
        self.sems.extend(sems)

    def block(self):
        return self.nc.Block()

    def __exit__(self, *exc):
        self.stack.__exit__(*exc)
        if exc[0] is None:
            self.nc.clear_and_free_semaphores(self.sems)
            self.nc.all_engine_barrier()
        return False


def load_mod_columns(sp, tr, layer, js, m, bcol, gcol, loaded):
    dr = tr.dram
    for s in range(2):
        for i, j in enumerate(js):
            if layer and s and j >= 2:
                continue
            sp.dma_start(m[:, s, i, :], tr.mod_raw[layer, s, j * D:(j + 1) * D].rearrange("(p k) -> p k", k=KD)) \
                .then_inc(loaded, 16)
    sp.dma_start(bcol[:], dr["b_mod"][layer, js[0] * D:(js[-1] + 1) * D].rearrange("(j p k) -> p j k", j=len(js), k=KD)) \
        .then_inc(loaded, 16)
    for i, n in enumerate(("g_mix_pre", "g_mix_post", "g_ffn_pre", "g_ffn_post")):
        sp.dma_start(gcol[:, i, :], dr[n][layer].rearrange("(p k) -> p k", k=KD)).then_inc(loaded, 16)


def start(tr):
    nc, dr = tr.nc, tr.dram
    N = 2 * D // 512
    with Phase(nc) as ph:
        w = [ph.sb(f"wmod{i}", [P, KD, 512]) for i in range(N)]
        c2 = ph.sb("c2", [P, 2, KD])
        bcol, gcol, m = ph.sb("bcol", [P, 2, KD]), ph.sb("gcol", [P, 4, KD]), ph.sb("m", [P, 2, 2, KD])
        rows = ph.sb("rows", [2, 2 * D])
        acc = [ph.ps(f"acc{i}", [2, 512]) for i in range(N)]
        no_token, sq, rt = ph.sb("no_token", [P, SLOTB]), ph.sb("sq", [P, D]), ph.sb("rt", [P, NT])
        h_loaded, filled, slots_cleared = ph.sem("h_loaded"), ph.sem("no_token_set"), ph.sem("slots_cleared")
        squared, rooted = ph.sem("squared"), ph.sem("rooted")
        c_loaded, w_loaded = ph.sem("c_loaded"), [ph.sem(f"w_loaded{i}") for i in range(N)]
        silu_done, mod_done, rows_done = ph.sem("silu_done"), ph.sem("mod_done"), ph.sem("rows_done")
        stored, loaded, biased = ph.sem("rows_stored"), ph.sem("columns_loaded"), ph.sem("biased")
        with ph.block() as block:
            @block.sync
            def _(sp):
                sp.dma_start(c2[:, 0, :], dr["c"].rearrange("o (p k) -> (o p) k", k=KD)).then_inc(c_loaded, 16)
                sp.dma_start(c2[:, 1, :], dr["c_ctx"].rearrange("(p k) -> p k", k=KD)).then_inc(c_loaded, 16)
                for i in range(N):
                    sp.dma_start(w[i][:], dr["w_mod"][0].rearrange("(p k) n -> p k n", k=KD)[:, :, i * 512:(i + 1) * 512]) \
                        .then_inc(w_loaded[i], 16)
                for t in range(NT):
                    src = dr["ctx"][0, t * P:(t + 1) * P, :] if t < CT else dr["x"][0, (t - CT) * P:(t - CT + 1) * P, :]
                    sp.dma_start(tr.h[:, t, :], src).then_inc(h_loaded, 16)
                sp.dma_start(tr.ident[:], dr["c_ident"]).then_inc(h_loaded, 16)
                sp.wait_ge(filled, 1)
                for layer in range(DEPTH):
                    sp.dma_start(tr.slot_name[layer].rearrange("(g r) o -> g (r o)", g=SLOTB), no_token[:]) \
                        .then_inc(slots_cleared, 16)
                sp.wait_ge(rows_done, N)
                for s in range(2):
                    sp.dma_start(tr.mod_raw[0, s:s + 1, 0:2 * D], rows[s:s + 1, :]).then_inc(stored, 16)
                sp.wait_ge(stored, 32)
                load_mod_columns(sp, tr, 0, (0, 1), m, bcol, gcol, loaded)
                sp.wait_ge(slots_cleared, 16 * DEPTH)

            @block.scalar
            def _(act):
                act.wait_ge(c_loaded, 32)
                nc.scalar.activation(tr.silu_c[:].rearrange("p k s -> p s k"), c2[:], ACT.Silu).then_inc(silu_done, 1)
                act.wait_ge(h_loaded, 16 * (NT + 1))
                for t in range(NT):
                    if t:
                        act.wait_ge(squared, t)
                    nc.scalar.activation(sq[:], tr.h[:, t, :], ACT.Square, accum_out=tr.h_ss[:, t:t + 1]) \
                        .then_inc(squared, 1)
                act.wait_ge(squared, NT)
                act.wait_ge(filled, 2)
                nc.scalar.activation(rt[:], tr.h_ss[:], ACT.Sqrt, bias=tr.eps[:, 0:1], scale=1.0 / D).then_inc(rooted, 1)

            @block.tensor
            def _(pe):
                pe.wait_ge(silu_done, 1)
                for i in range(N):
                    pe.wait_ge(w_loaded[i], 16)
                    for k in range(KD):
                        mm = nc.tensor.matmul(acc[i][:], tr.silu_c[:, k, :], w[i][:, k, :],
                                              start=(k == 0), stop=(k == KD - 1))
                    mm.then_inc(mod_done, 1)

            @block.vector
            def _(dve):
                nc.vector.memset(no_token[:], float(T * TOPK)).then_inc(filled, 1)
                nc.vector.memset(tr.eps[:], EPS).then_inc(filled, 1)
                nc.vector.memset(tr.ones[:], 1.0)
                for i in range(N):
                    dve.wait_ge(mod_done, i + 1)
                    nc.vector.tensor_copy(rows[:, i * 512:(i + 1) * 512], acc[i][:]).then_inc(rows_done, 1)
                dve.wait_ge(rooted, 1)
                nc.vector.reciprocal(tr.h_rs[:], rt[:])
                dve.wait_ge(loaded, 16 * 9)
                pre_columns(dve, tr, 0, m, bcol, gcol, biased)


def pre_columns(dve, tr, layer, m, bcol, gcol, biased):
    nc = tr.nc
    for s in range(2):
        nc.vector.tensor_tensor(m[:, s, 0:2], m[:, s, 0:2], bcol[:, 0:2, :], ALU.add).then_inc(biased, 1)
    dve.wait_ge(biased, 2)
    for s in range(2):
        nc.vector.scalar_tensor_tensor(tr.pre_scale[:, layer, :, s], m[:, s, 1, :], 1.0, gcol[:, 0, :],
                                       ALU.add, ALU.mult)
        nc.vector.tensor_copy(tr.pre_shift[:, layer, :, s], m[:, s, 0, :])


class ModulationEnd:

    def __init__(self, tr, ph):
        self.tr, self.nc = tr, tr.nc
        self.bcol = [ph.sb(f"mod_bcol{i}", [P, 6 - 2 * (i == 0), KD]) for i in range(DEPTH)]
        self.gcol = [ph.sb(f"mod_gcol{i}", [P, 4, KD]) for i in range(DEPTH)]
        self.m = [ph.sb(f"mod_m{i}", [P, 2, 6 - 2 * (i == 0), KD]) for i in range(DEPTH)]
        self.rows = [ph.sb(f"mod_rows{i}", [P, 4, 2, KD]) for i in range(DEPTH)]
        self.loaded = [ph.sem(f"mod_loaded{i}") for i in range(DEPTH)]
        self.biased, self.pre_biased = ph.sem("mod_biased"), ph.sem("mod_pre_biased")
        self.rows_done, self.stored = ph.sem("mod_rows_done"), ph.sem("mod_rows_stored")

    def sync(self, sp):
        load_mod_columns(sp, self.tr, 0, (2, 3, 4, 5), self.m[0], self.bcol[0], self.gcol[0], self.loaded[0])
        load_mod_columns(sp, self.tr, 1, (0, 1, 2, 3, 4, 5), self.m[1], self.bcol[1], self.gcol[1], self.loaded[1])
        n = 0
        for layer in range(DEPTH):
            for s in range(2 - layer):
                sp.wait_ge(self.rows_done, 4 * (n // 4 + 1))
                for i in range(4):
                    sp.dma_start(self.tr.mod_row[layer, i, s, :].rearrange("(p k) -> p k", k=KD),
                                 self.rows[layer][:, i, s, :]).then_inc(self.stored, 16)
                    n += 1
        sp.wait_ge(self.stored, 16 * n)

    def vector(self, dve):
        n = 0
        for layer in range(DEPTH):
            at = 2 * layer
            dve.wait_ge(self.loaded[layer], 16 * 13)
            mv, bv, gv = self.m[layer], self.bcol[layer], self.gcol[layer]
            if layer:
                pre_columns(dve, self.tr, 1, mv, bv, gv, self.pre_biased)
            for s in range(2 - layer):
                self.nc.vector.tensor_tensor(mv[:, s, at:at + 4], mv[:, s, at:at + 4], bv[:, at:at + 4, :], ALU.add) \
                    .then_inc(self.biased, 1)
                n += 1
                dve.wait_ge(self.biased, n)
                gate_a, shift_f, scale_f, gate_f = (mv[:, s, at + i, :] for i in range(4))
                r = self.rows[layer]
                self.nc.vector.tensor_tensor(r[:, 0, s, :], gate_a, gv[:, 1, :], ALU.mult).then_inc(self.rows_done, 1)
                self.nc.vector.scalar_tensor_tensor(r[:, 1, s, :], scale_f, 1.0, gv[:, 2, :], ALU.add, ALU.mult) \
                    .then_inc(self.rows_done, 1)
                self.nc.vector.tensor_copy(r[:, 2, s, :], shift_f).then_inc(self.rows_done, 1)
                self.nc.vector.tensor_tensor(r[:, 3, s, :], gate_f, gv[:, 3, :], ALU.mult).then_inc(self.rows_done, 1)


def norm_transpose(tr, layer, uT, load_ahead):
    nc = tr.nc
    with Phase(nc) as ph:
        xn = [ph.sb(f"xn{i}", [P, D]) for i in range(2)]
        pt = [ph.ps(f"pt{i}", [P, 4, P]) for i in range(4)]
        scaled, turned, placed = ph.sem("scaled"), ph.sem("turned"), ph.sem("placed")
        placed_v = ph.sem("placed_v")
        with ph.block() as block:
            @block.sync
            def _(sp):
                load_ahead(sp)

            @block.scalar
            def _(act):
                for t in range(NT):
                    s = 1 if t < CT else 0
                    act.wait_ge(turned, 2 * t + 2)
                    for k in range(4, 8):
                        nc.scalar.activation(uT[:, k, t * P:(t + 1) * P], pt[(2 * t + 1) % 4][:, k - 4, :],
                                             ACT.Identity, bias=tr.pre_shift[:, layer, k, s:s + 1],
                                             scale=tr.pre_scale[:, layer, k, s:s + 1]).then_inc(placed, 1)

            @block.vector
            def _(dve):
                def scale(t):
                    if t >= 2:
                        dve.wait_ge(turned, 2 * (t - 1))
                    nc.vector.tensor_scalar(xn[t % 2][:], tr.h[:, t, :], tr.h_rs[:, t:t + 1], None, ALU.mult) \
                        .then_inc(scaled, 1)

                scale(0)
                for t in range(NT):
                    if t + 1 < NT:
                        scale(t + 1)
                    s = 1 if t < CT else 0
                    dve.wait_ge(turned, 2 * t + 1)
                    for k in range(4):
                        nc.vector.tensor_scalar(uT[:, k, t * P:(t + 1) * P], pt[(2 * t) % 4][:, k, :],
                                                tr.pre_scale[:, layer, k, s:s + 1], tr.pre_shift[:, layer, k, s:s + 1],
                                                ALU.mult, ALU.add).then_inc(placed_v, 1)

            @block.tensor
            def _(pe):
                for t in range(NT):
                    pe.wait_ge(scaled, t + 1)
                    for half in range(2):
                        if t >= 2:
                            pe.wait_ge(placed if half else placed_v, 4 * (t - 1))
                        for k in range(4):
                            mm = nc.tensor.transpose(pt[(2 * t + half) % 4][:, k, :],
                                                     xn[t % 2][:, half * 4 + k:D:KD], tr.ident[:])
                        mm.then_inc(turned, 1)


class Drains:

    def __init__(self, engines):
        self.engines = engines

    def count(self, n, engine):
        return sum(e == engine for e in self.engines[:n])


EVEN_GROUPS = [(Q0, V0), (A0, SK0), (SK0, EVEN_IN), (V0, G0), (G0, A0)]


def load_group(eng, tr, w, w_loaded, g):
    w_dram = tr.dram["w_in_e"][0].rearrange("(p k) n -> p k n", k=KD)
    a, b = EVEN_GROUPS[g]
    if g == 2:
        for i in range(2 * SKV):
            src = SK0 + (i // 2) * SHD
            eng.dma_start(w[0][:, :, i * SHD:(i + 1) * SHD], w_dram[:, :, src:src + SHD]).then_inc(w_loaded[0], 16)
        eng.dma_start(w[0][:, :, 2 * P:2 * P + EVEN_IN - SV0], w_dram[:, :, SV0:EVEN_IN]).then_inc(w_loaded[0], 16)
    else:
        eng.dma_start(w[g % 2][:, :, 0:b - a], w_dram[:, :, a:b]).then_inc(w_loaded[g % 2], 16)


def even_project(tr, uT, qkT, aT, sqT, skT, v, gs, sv, spare, w, w_loaded):
    nc, dr = tr.nc, tr.dram
    HALF = T // 2
    GROUPS = EVEN_GROUPS
    jobs = []
    jobs += [(0, "qk", i, hf) for i in range(4) for hf in range(2)]
    jobs += [(1, "a", 0, hf) for hf in range(2)]
    jobs += [(1, "sq", i, hf) for i in range(4) for hf in range(2)]
    jobs += [(2, "sk", i, hf) for i in range(2) for hf in range(2)]
    jobs += [(2, "sv", 0, t) for t in range(NT)]
    jobs += [(3, "v", 0, t) for t in range(NT)]
    jobs += [(4, "g", 0, t) for t in range(NT)]
    engines = ["act" for _ in jobs]
    drains = Drains(engines)
    NB = 6
    MC, MBUF, ABUF = 256, 5, 4
    slices = [(0, n) for n in range(2 * D // MC, 6 * D // MC)] + [(1, n) for n in range(6 * D // MC)]
    items = [(i, s) for i, (layer, n) in enumerate(slices) for s in range(1 if layer and n >= 2 * D // MC else 2)]
    last_item = [max(m for m, (i, _) in enumerate(items) if i == j) + 1 for j in range(len(slices))]
    slots = len(jobs) - 3
    in_slot = [[m for m in range(len(items)) if m // 2 * slots // (len(items) // 2) == n] for n in range(len(jobs))]
    runs = [(layer, s, [m for m, (i, x) in enumerate(items) if (slices[i][0], x) == (layer, s)])
            for layer in range(DEPTH) for s in range(2)]
    HALVES = MC // P
    column = {m: HALVES * n for n, m in enumerate(m for _, _, ms in runs for m in ms)}
    loads = [1, 1, 1 + 2 * SKV + 1, 2, 1 + 2 * SKV + 1 + 1]
    last_of = [max(n for n, j in enumerate(jobs) if j[0] == g) + 1 for g in range(len(GROUPS))]
    with Phase(nc) as ph:
        ph.adopt(w_loaded)
        bank = [ph.ps(f"bank{i}", [P, 512]) for i in range(NB)]
        product, read_dve, read_act = ph.sem("product"), ph.sem("read_dve"), ph.sem("read_act")
        wm = [ph.sb(f"wm{i}", [P, KD, MC])[:] for i in range(MBUF - 2)]
        wm += [spare[:, 2 * i:2 * i + 2, :].rearrange("p t (k n) -> p (t k) n", n=MC) for i in range(2)]
        part = [ph.sb(f"part{i}", [P, MC]) for i in range(ABUF)]
        columns, mrows = (spare[:, 4, i * P:(i + 1) * P] for i in range(2))
        mcols, mturn = ph.ps("mcols", [P, P]), ph.ps("mturn", [P, P])
        wm_loaded = [ph.sem(f"wm_loaded{i}") for i in range(MBUF)]
        term, part_done, reduced = ph.sem("term"), ph.sem("part_done"), ph.sem("reduced")
        copied, mod_turned, mod_rows = ph.sem("mod_copied"), ph.sem("mod_turned"), ph.sem("mod_rows")
        stored = ph.sem("mod_stored")

        def target(kind, i, x):
            cols = slice(x * HALF, (x + 1) * HALF)
            if kind == "qk":
                return qkT[:, i, cols], P, HALF
            if kind == "a":
                return aT[:, cols], 2 * GRANK, HALF
            if kind == "sq":
                return sqT[:, i, cols], P, HALF
            if kind == "sk":
                return skT[:, i, cols], P, HALF
            if kind == "sv":
                return sv[:, x, :], P, SKV * SHD
            return (v if kind == "v" else gs)[:, x, :], P, GH * GDV

        with ph.block() as block:
            @block.sync
            def _(sp):
                sp.wait_ge(mod_rows, 1)
                for layer, s, ms in runs:
                    r, lo = column[ms[0]], slices[items[ms[0]][0]][1] * MC
                    sp.dma_start(tr.mod_raw[layer, s, lo:lo + len(ms) * MC].rearrange("(r c) -> r c", c=P),
                                 mrows[r:r + HALVES * len(ms), :]).then_inc(stored, 16)
                sp.wait_ge(stored, 16 * len(runs))

            @block.gpsimd
            def _(pool):
                for i, (layer, n) in enumerate(slices):
                    if i >= MBUF:
                        pool.wait_ge(part_done, last_item[i - MBUF])
                    pool.dma_start(wm[i % MBUF], dr["w_mod"][layer].rearrange("(p k) n -> p k n", k=KD)
                                   [:, :, n * MC:(n + 1) * MC]).then_inc(wm_loaded[i % MBUF], 16)

            @block.tensor
            def _(pe):
                for n, (g, kind, i, x) in enumerate(jobs):
                    wt = w[g % 2]
                    if n == 0 or jobs[n - 1][0] != g:
                        pe.wait_ge(w_loaded[g % 2], 16 * loads[g])
                    if n >= NB:
                        e = engines[n - NB]
                        pe.wait_ge(read_dve if e == "dve" else read_act, drains.count(n - NB + 1, e))
                    _, m, cnt = target(kind, i, x)
                    o = bank[n % NB][0:m, 0:cnt]
                    for k in range(KD):
                        if kind in ("qk", "a", "sq", "sk"):
                            rhs = uT[:, k, x * HALF:(x + 1) * HALF]
                            if kind == "qk":
                                lhs = wt[:, k, i * P:(i + 1) * P]
                            elif kind == "a":
                                lhs = wt[:, k, 0:2 * GRANK]
                            elif kind == "sq":
                                lhs = wt[:, k, SQ0 - A0 + i * P:SQ0 - A0 + (i + 1) * P]
                            else:
                                lhs = wt[:, k, i * P:(i + 1) * P]
                        else:
                            lhs = uT[:, k, x * P:(x + 1) * P]
                            rhs = wt[:, k, 2 * P:2 * P + cnt] if kind == "sv" else wt[:, k, 0:cnt]
                        mm = nc.tensor.matmul(o, lhs, rhs, start=(k == 0), stop=(k == KD - 1))
                    mm.then_inc(product, 1)
                    for m in in_slot[n - 1] if n else []:
                        pe.wait_ge(part_done, m + 1)
                        for i in range(HALVES):
                            mm = nc.tensor.matmul(mcols[:, column[m] + i:column[m] + i + 1],
                                                  part[m % ABUF][:, i * P:(i + 1) * P], tr.ones[:, 0:1],
                                                  start=True, stop=True)
                        mm.then_inc(reduced, 1)
                    if n == slots + 1:
                        pe.wait_ge(copied, 1)
                        nc.tensor.transpose(mturn[:], columns, tr.ident[:]).then_inc(mod_turned, 1)

            @block.vector
            def _(dve):
                for n, (g, kind, i, x) in enumerate(jobs):
                    pair = in_slot[n]
                    for m in pair:
                        sl = items[m][0]
                        dve.wait_ge(wm_loaded[sl % MBUF], 16 * (sl // MBUF + 1))
                        if m >= ABUF:
                            dve.wait_ge(reduced, m - ABUF + 1)
                    for k in range(KD):
                        for m in pair:
                            sl, s = items[m]
                            acc, c = part[m % ABUF][:], tr.silu_c[:, k, s:s + 1]
                            if k == 0:
                                ins = nc.vector.tensor_scalar(acc, wm[sl % MBUF][:, k, :], c, None, ALU.mult)
                            else:
                                dve.wait_ge(term, m // 2 * 2 * (KD - 1) + 2 * (k - 1) + m % 2 + 1)
                                ins = nc.vector.scalar_tensor_tensor(acc, wm[sl % MBUF][:, k, :], c, acc,
                                                                     ALU.mult, ALU.add)
                            ins.then_inc(term if k < KD - 1 else part_done, 1)
                    if n == slots + 1:
                        dve.wait_ge(reduced, len(items))
                        nc.vector.tensor_copy(columns, mcols[:]).then_inc(copied, 1)
                        dve.wait_ge(mod_turned, 1)
                        nc.vector.tensor_copy(mrows, mturn[:]).then_inc(mod_rows, 1)
                    if engines[n] == "dve":
                        dst, m, cnt = target(kind, i, x)
                        dve.wait_ge(product, n + 1)
                        nc.vector.tensor_copy(dst, bank[n % NB][0:m, 0:cnt]).then_inc(read_dve, 1)

            @block.scalar
            def _(act):
                for n, (g, kind, i, x) in enumerate(jobs):
                    for later in range(2, len(GROUPS)):
                        if n == last_of[later - 2]:
                            act.wait_ge(product, n)
                            load_group(act, tr, w, w_loaded, later)
                    if engines[n] == "act":
                        dst, m, cnt = target(kind, i, x)
                        act.wait_ge(product, n + 1)
                        nc.scalar.activation(dst, bank[n % NB][0:m, 0:cnt], ACT.Silu if kind == "g" else ACT.Copy) \
                            .then_inc(read_act, 1)


ORDER = [list(range(NT)), list(range(CT))[::-1] + list(range(CT, NT))[::-1]]
MID = P // 2 - 1


def gla_decays(tr, qkT, aT, qa, kb, carry):
    nc, dr = tr.nc, tr.dram
    HALF = T // 2
    with Phase(nc) as ph:
        wa = ph.sb("wa", [2 * GRANK, 2, GH * GDK])
        ba = ph.sb("ba", [P, 4])
        reset = ph.sb("reset", [P, T])
        mid, total = ph.sb("mid", [P, 4, NT]), ph.sb("total", [P, 4, NT])
        low = [ph.ps(f"low{i}", [P, 512]) for i in range(8)]
        loaded, cleared, logits = ph.sem("wa2_loaded"), ph.sem("cleared"), ph.sem("logits")
        split, absed, exped, logged = ph.sem("z_split"), ph.sem("absed"), ph.sem("exped"), ph.sem("logged")
        decay, summed, mids = ph.sem("decay_done"), ph.sem("summed"), ph.sem("mids_done")
        relative, carried = ph.sem("relative_done"), ph.sem("carry_summed")
        factor_q, factor_k, carry_done = ph.sem("factor_q"), ph.sem("factor_k"), ph.sem("carry_done")
        products = ph.sem("products_done")
        with ph.block() as block:
            @block.sync
            def _(sp):
                sp.wait_ge(cleared, 1)
                for d in range(2):
                    sp.dma_start(wa[d * GRANK:(d + 1) * GRANK, d, :], dr["gla_wa2"][0, d]).then_inc(loaded, 16)
                    sp.dma_start(ba[:, 2 * d:2 * d + 2], dr["gla_ba"][0, d].rearrange("(j p) -> p j", p=P),
                                 allow_slow_non_contiguous=True) \
                        .then_inc(loaded, 16)

            @block.tensor
            def _(pe):
                pe.wait_ge(loaded, 64)
                for x in range(4):
                    for hf in range(2):
                        mm = nc.tensor.matmul(low[2 * x + hf][:, 0:HALF], wa[:, x // 2, (x % 2) * P:(x % 2 + 1) * P],
                                              aT[:, hf * HALF:(hf + 1) * HALF], start=True, stop=True)
                    mm.then_inc(logits, 1)

            @block.vector
            def _(dve):
                nc.vector.memset(wa[:], 0.0).then_inc(cleared, 1)
                nc.vector.memset(reset[:], 1.0).then_inc(cleared, 1)
                dve.wait_ge(cleared, 2)
                nc.vector.memset(reset[:, 0:T:P], 0.0).then_inc(cleared, 1)
                dve.wait_ge(loaded, 64)
                for x in range(4):
                    dve.wait_ge(absed, 2 * x + 2)
                    for hf in range(2):
                        cols = slice(hf * HALF, (hf + 1) * HALF)
                        z = low[2 * x + hf][:, 0:HALF]
                        nc.vector.tensor_scalar(kb[:, x, cols], z, ba[:, x:x + 1], 0.0, ALU.add, ALU.min) \
                            .then_inc(split, 1)
                dve.wait_ge(cleared, 3)
                dve.wait_ge(split, 8)
                for x in range(4):
                    dve.wait_ge(logged, x + 1)
                    nc.vector.tensor_tensor(kb[:, x, :], kb[:, x, :], qa[:, x, :], ALU.subtract).then_inc(decay, 1)
                    dve.wait_ge(decay, x + 1)
                    nc.vector.tensor_tensor_scan(qa[:, x, :], reset[:], kb[:, x, :], 0.0, ALU.mult, ALU.add) \
                        .then_inc(summed, 1)
                dve.wait_ge(summed, 4)
                cum = qa[:].rearrange("p x (c i) -> p x c i", i=P)
                rel = kb[:].rearrange("p x (c i) -> p x c i", i=P)
                nc.vector.tensor_copy(total[:], cum[:, :, :, P - 1]).then_inc(mids, 1)
                nc.vector.tensor_copy(mid[:, 0:2, :], cum[:, 0:2, :, MID]).then_inc(mids, 1)
                nc.vector.tensor_tensor(kb[:, 2:4, :], kb[:, 2:4, :], qa[:, 2:4, :], ALU.subtract) \
                    .then_inc(relative, 1)
                dve.wait_ge(relative, 1)
                nc.vector.tensor_copy(mid[:, 2:4, :], rel[:, 2:4, :, MID]).then_inc(mids, 1)
                dve.wait_ge(mids, 3)
                for x in range(4):
                    src = cum if x < 2 else rel
                    nc.vector.tensor_tensor(rel[:, x], src[:, x], mid[:, x, :].unsqueeze(2).to_broadcast([P, NT, P]),
                                            ALU.subtract).then_inc(relative, 1)
                n = 0
                for d in range(2):
                    for a, b in zip(ORDER[d], ORDER[d][1:]):
                        xs = slice(2 * d, 2 * d + 2)
                        nc.vector.tensor_tensor(carry[:, d, b, :], mid[:, xs, b], mid[:, xs, a], ALU.subtract) \
                            .then_inc(carried, 1)
                        n += 1
                        dve.wait_ge(carried, n)
                        tot = a if d == 0 else b
                        nc.vector.tensor_tensor(carry[:, d, b, :], carry[:, d, b, :], total[:, xs, tot], ALU.add) \
                            .then_inc(carried, 1)
                        n += 1
                for x in range(4):
                    dve.wait_ge(factor_q, x + 1)
                    nc.vector.scalar_tensor_tensor(qa[:, x, :], qkT[:, x % 2, :], float(GDK ** -0.5), qa[:, x, :],
                                                   ALU.mult, ALU.mult).then_inc(products, 1)

            @block.gpsimd
            def _(pool):
                for x in range(4):
                    pool.wait_ge(factor_k, x + 1)
                    nc.gpsimd.tensor_tensor(kb[:, x, :], kb[:, x, :], qkT[:, 2 + x % 2, :], ALU.mult) \
                        .then_inc(products, 1)

            @block.scalar
            def _(act):
                act.wait_ge(loaded, 64)
                for x in range(4):
                    act.wait_ge(logits, x + 1)
                    for hf in range(2):
                        nc.scalar.activation(qa[:, x, hf * HALF:(hf + 1) * HALF], low[2 * x + hf][:, 0:HALF],
                                             ACT.Abs, bias=ba[:, x:x + 1]).then_inc(absed, 1)
                for x in range(4):
                    act.wait_ge(absed, 2 * x + 2)
                    nc.scalar.activation(qa[:, x, :], qa[:, x, :], ACT.Exp, scale=-1.0).then_inc(exped, 1)
                for x in range(4):
                    act.wait_ge(exped, x + 1)
                    nc.scalar.activation(qa[:, x, :], qa[:, x, :], ACT.Ln, bias=tr.ones[:, 0:1]).then_inc(logged, 1)
                for x in range(4):
                    act.wait_ge(relative, x + 2)
                    nc.scalar.activation(qa[:, x, :], kb[:, x, :], ACT.Exp, scale=1.0 / GTAU).then_inc(factor_q, 1)
                    act.wait_ge(factor_q, x + 1)
                    nc.scalar.activation(kb[:, x, :], kb[:, x, :], ACT.Exp, scale=-1.0 / GTAU).then_inc(factor_k, 1)
                act.wait_ge(carried, 4 * (NT - 1))
                for d in range(2):
                    b = ORDER[d][0]
                    for lo, hi in ((0, b), (b + 1, NT)):
                        if lo < hi:
                            nc.scalar.activation(carry[:, d, lo:hi, :], carry[:, d, lo:hi, :], ACT.Exp,
                                                 scale=1.0 / GTAU).then_inc(carry_done, 1)


def gla_states(tr, kb, v, carry, sm):
    nc = tr.nc
    with Phase(nc) as ph:
        kbt = ph.sb("kbt", [P, NT, 4, P])
        t = ph.sb("t", [P, 2, 2, GDV])
        turn = [ph.ps(f"turn{i}", [P, 4, P]) for i in range(2)]
        gain = [ph.ps(f"gain{i}", [P, 4, GDV]) for i in range(NT)]
        turned, placed, gained = ph.sem("keys_turned"), ph.sem("keys_placed"), ph.sem("gained")
        added, state = ph.sem("gain_added"), ph.sem("state_done")
        with ph.block() as block:
            @block.tensor
            def _(pe):
                def turn_keys(c):
                    if c >= 2:
                        pe.wait_ge(placed, c - 1)
                    for x in range(4):
                        mm = nc.tensor.transpose(turn[c % 2][:, x, :], kb[:, x, c * P:(c + 1) * P], tr.ident[:])
                    mm.then_inc(turned, 1)

                turn_keys(0)
                for c in range(NT):
                    if c + 1 < NT:
                        turn_keys(c + 1)
                    pe.wait_ge(placed, c + 1)
                    for x in range(4):
                        for i in range(2):
                            head = 2 * (x % 2) + i
                            mm = nc.tensor.matmul(gain[c][i * GDK:(i + 1) * GDK, x, :],
                                                  kbt[:, c, x, i * GDK:(i + 1) * GDK],
                                                  v[:, c, head * GDV:(head + 1) * GDV], start=True, stop=True)
                    mm.then_inc(gained, 1)

            @block.scalar
            def _(act):
                for c in range(NT):
                    act.wait_ge(turned, c + 1)
                    nc.scalar.copy(kbt[:, c, :, :], turn[c % 2][:]).then_inc(placed, 1)

            @block.vector
            def _(dve):
                dve.wait_ge(gained, NT)
                for s in range(NT - 1):
                    for d in range(2):
                        a, b = ORDER[d][s], ORDER[d][s + 1]
                        xs = slice(2 * d, 2 * d + 2)
                        g = gain[a][:, xs, :]
                        if s:
                            dve.wait_ge(state, 2 * (s - 1) + d + 1)
                            nc.vector.tensor_tensor(t[:, d], sm[:, a, xs, :], g, ALU.add).then_inc(added, 1)
                            dve.wait_ge(added, 2 * (s - 1) + d + 1)
                            g = t[:, d]
                        f = carry[:, d, b, :].unsqueeze(2).to_broadcast([P, 2, GDV])
                        nc.vector.tensor_tensor(sm[:, b, xs, :], g, f, ALU.mult).then_inc(state, 1)


def gla_outputs(tr, qa, kb, v, sm, gs, cat):
    nc, dr = tr.nc, tr.dram
    with Phase(nc) as ph:
        st = [[ph.sb(f"st{i}{d}", [P, GH, P]) for d in range(2)] for i in range(2)]
        norm = ph.sb("norm", [P, GDV])
        mask = ph.sb("mask", [P, 2, P])
        sq = ph.sb("sq", [P, GH, GDV])
        ss, rt, rs = ph.sb("ss", [P, NT, GH]), ph.sb("rt", [P, NT, GH]), ph.sb("rs", [P, NT, GH])
        sc = [[ph.ps(f"sc{i}{d}", [P, GH, P]) for d in range(2)] for i in range(2)]
        op = [[ph.ps(f"o{i}{d}", [P, 2, GDV]) for d in range(2)] for i in range(2)]
        loaded, scored, masked = ph.sem("loaded"), ph.sem("scored"), ph.sem("masked")
        out_done, out_read, squared = ph.sem("out_done"), ph.sem("out_read"), ph.sem("squared")
        reduced, rooted, inverted = ph.sem("reduced"), ph.sem("rooted"), ph.sem("inverted")
        gated, normed = ph.sem("gated"), ph.sem("normed")
        modulation = ModulationEnd(tr, ph)
        with ph.block() as block:
            @block.sync
            def _(sp):
                sp.dma_start(mask[:], dr["c_causal"]).then_inc(loaded, 16)
                sp.dma_start(norm[:], dr["gla_norm"].to_broadcast([P, GDV])).then_inc(loaded, 16)
                modulation.sync(sp)

            @block.tensor
            def _(pe):
                def scores(c):
                    if c >= 2:
                        pe.wait_ge(masked, 2 * (c - 1))
                    for i in range(2):
                        r, cols = slice(i * GDK, (i + 1) * GDK), slice(c * P, (c + 1) * P)
                        for x in range(4):
                            mm = nc.tensor.matmul(sc[c % 2][i][:, x, :], kb[r, x, cols], qa[r, x, cols],
                                                  start=True, stop=True)
                        mm.then_inc(scored, 1)

                scores(0)
                for c in range(NT):
                    if c + 1 < NT:
                        scores(c + 1)
                    pe.wait_ge(masked, 2 * (c + 1))
                    if c >= 2:
                        pe.wait_ge(out_read, 2 * (c - 1))
                    cols = slice(c * P, (c + 1) * P)
                    for head in range(GH):
                        r = slice((head % 2) * GDK, (head % 2 + 1) * GDK)
                        terms = []
                        for d in range(2):
                            terms.append((st[c % 2][head % 2][:, 2 * d + head // 2, :], v[:, c, head * GDV:(head + 1) * GDV]))
                            if c != ORDER[d][0]:
                                x = 2 * d + head // 2
                                terms.append((qa[r, x, cols], sm[r, c, x, :]))
                        for n, (a, b) in enumerate(terms):
                            mm = nc.tensor.matmul(op[c % 2][head % 2][:, head // 2, :], a, b, start=(n == 0),
                                                  stop=(n == len(terms) - 1))
                    mm.then_inc(out_done, 1)

            @block.vector
            def _(dve):
                dve.wait_ge(loaded, 32)

                def mask_scores(c):
                    if c >= 2:
                        dve.wait_ge(out_done, c - 1)
                    for i in range(2):
                        dve.wait_ge(scored, 2 * c + i + 1)
                        nc.vector.tensor_tensor(st[c % 2][i][:].rearrange("p (d j) n -> p d j n", d=2),
                                                sc[c % 2][i][:].rearrange("p (d j) n -> p d j n", d=2),
                                                mask[:].unsqueeze(2).to_broadcast([P, 2, 2, P]), ALU.mult) \
                            .then_inc(masked, 1)

                mask_scores(0)
                for c in range(NT):
                    if c + 1 < NT:
                        mask_scores(c + 1)
                    o = cat[:, c, 0:GH * GDV].rearrange("p (h e) -> p h e", h=GH)
                    dve.wait_ge(out_read, 2 * (c + 1))
                    if c:
                        dve.wait_ge(reduced, c)
                    nc.vector.tensor_tensor(sq[:], o, o, ALU.mult).then_inc(squared, 1)
                    dve.wait_ge(squared, c + 1)
                    nc.vector.reduce_sum(ss[:, c, :], sq[:], AX).then_inc(reduced, 1)
                    if c == 2:
                        modulation.vector(dve)
                dve.wait_ge(rooted, 1)
                nc.vector.reciprocal(rs[:], rt[:]).then_inc(inverted, 1)
                dve.wait_ge(inverted, 1)
                for c in range(NT):
                    o = cat[:, c, 0:GH * GDV].rearrange("p (h e) -> p h e", h=GH)
                    nc.vector.tensor_tensor(o, o, rs[:, c, :].unsqueeze(2).to_broadcast([P, GH, GDV]), ALU.mult) \
                        .then_inc(normed, 1)
                for c in range(NT):
                    o = cat[:, c, 0:GH * GDV]
                    dve.wait_ge(normed, c + 1)
                    dve.wait_ge(gated, c + 1)
                    nc.vector.tensor_tensor(o, o, gs[:, c, :], ALU.mult)

            @block.scalar
            def _(act):
                for c in range(NT):
                    act.wait_ge(out_done, c + 1)
                    o = cat[:, c, 0:GH * GDV].rearrange("p (j i e) -> p i j e", i=2, e=GDV)
                    for i in range(2):
                        nc.scalar.copy(o[:, i], op[c % 2][i][:]).then_inc(out_read, 1)
                act.wait_ge(reduced, NT)
                nc.scalar.activation(rt[:], ss[:], ACT.Sqrt, bias=tr.eps[:, 0:1], scale=1.0 / GDV).then_inc(rooted, 1)

            @block.gpsimd
            def _(pool):
                pool.wait_ge(loaded, 32)
                for c in range(NT):
                    g = gs[:, c, :].rearrange("p (h e) -> p h e", h=GH)
                    nc.gpsimd.tensor_tensor(g, g, norm[:].unsqueeze(1).to_broadcast([P, GH, GDV]), ALU.mult) \
                        .then_inc(gated, 1)


def rotate(tr, parts):
    nc, dr = tr.nc, tr.dram
    N = len(parts)
    with Phase(nc) as ph:
        rope = ph.sb("rope", [P, 2, NLAT])
        swap = ph.sb("swap", [P, P])
        part = ph.sb("part", [P, 2, NLAT])
        bank = [ph.ps(f"bank{i}", [P, NLAT]) for i in range(4)]
        loaded, swapped, sines = ph.sem("loaded"), ph.sem("swapped"), ph.sem("sines")
        cosines, rotated = ph.sem("cosines"), ph.sem("rotated")
        with ph.block() as block:
            @block.sync
            def _(sp):
                sp.dma_start(rope[:], dr["c_rope"]).then_inc(loaded, 16)
                sp.dma_start(swap[:], dr["c_swap"]).then_inc(loaded, 16)

            @block.tensor
            def _(pe):
                pe.wait_ge(loaded, 32)
                for n, x in enumerate(parts):
                    if n >= 4:
                        pe.wait_ge(sines, n - 3)
                    nc.tensor.matmul(bank[n % 4][:], swap[:], x, start=True, stop=True).then_inc(swapped, 1)

            @block.gpsimd
            def _(pool):
                pool.wait_ge(loaded, 32)
                for n, x in enumerate(parts):
                    pool.wait_ge(swapped, n + 1)
                    nc.gpsimd.tensor_tensor(x, x, rope[:, 0, :], ALU.mult).then_inc(cosines, 1)

            @block.vector
            def _(dve):
                dve.wait_ge(loaded, 32)
                for n, x in enumerate(parts):
                    dve.wait_ge(swapped, n + 1)
                    if n >= 2:
                        dve.wait_ge(rotated, n - 1)
                    nc.vector.tensor_tensor(part[:, n % 2, :], bank[n % 4][:], rope[:, 1, :], ALU.mult) \
                        .then_inc(sines, 1)
                    dve.wait_ge(sines, n + 1)
                    dve.wait_ge(cosines, n + 1)
                    nc.vector.tensor_tensor(x, x, part[:, n % 2, :], ALU.add).then_inc(rotated, 1)


def window_attention(tr, sqT, skT, sv, cat, load_ahead):
    nc, dr = tr.nc, tr.dram
    NK = NCTX + 3 * P
    scale = float(SHD ** -0.5)

    def keys(t):
        if t < CT:
            return list(range(CT)), 0
        near = [j for j in (t - 1, t, t + 1) if CT <= j < NT]
        return list(range(CT)) + near, (1 if t == CT else 0)

    with Phase(nc) as ph:
        s = [ph.sb(f"s{i}", [P, SH, NK]) for i in range(2)]
        pT = ph.sb("pT", [P, CT + 3, SH, P])
        mask = ph.sb("mask", [P, 2, NK])
        sink = ph.sb("sink", [P, SH])
        top, m, nm = ph.sb("top", [P, NT, SH]), ph.sb("m", [P, NT, SH]), ph.sb("nm", [P, NT, SH])
        es, total, den = ph.sb("es", [P, NT, SH]), ph.sb("total", [P, NT, SH]), ph.sb("den", [P, NT, SH])
        rden, ed = ph.sb("rden", [P, NT, SH]), ph.sb("ed", [P, NT, SH])
        raw = [ph.ps(f"raw{i}", [P, 1024]) for i in range(2)]
        turn = [ph.ps(f"turn{i}", [P, 4, P]) for i in range(2)]
        op = [ph.ps(f"op{i}", [P, SH, SHD]) for i in range(2)]
        loaded, scored, masked = ph.sem("loaded"), ph.sem("scored"), ph.sem("masked")
        maxed, negated, probs = ph.sem("maxed"), ph.sem("negated"), ph.sem("probs_ready")
        diff, sinks, summed, inverted = ph.sem("diff"), ph.sem("sinks"), ph.sem("summed"), ph.sem("inverted")
        turned, placed_v, placed_a = ph.sem("turned"), ph.sem("placed_v"), ph.sem("placed_a")
        attended, normed = ph.sem("attended"), ph.sem("normed")
        quads = [(t, b, q) for t in range(NT) for q in range(2) for b in range(len(keys(t)[0]))]
        LAG = 2

        def before(t):
            return sum(2 * len(keys(i)[0]) for i in range(t))

        def steps(t):
            n = before(t + 1) - before(t)
            for i in range(max(SH, n + LAG)):
                yield (i if i < SH and t + 1 < NT else None), (before(t) + i - LAG if LAG <= i < n + LAG else None)

        with ph.block() as block:
            @block.sync
            def _(sp):
                sp.dma_start(mask[:], dr["c_band"]).then_inc(loaded, 16)
                sp.dma_start(sink[:], dr["swa_sink"].to_broadcast([P, SH])).then_inc(loaded, 16)
                load_ahead(sp)

            @block.tensor
            def _(pe):
                def score(t, head):
                    near = keys(t)[0][CT:]
                    n = t * SH + head
                    if n >= 2:
                        pe.wait_ge(masked, n - 1)
                    r = slice((head % 2) * SHD, (head % 2 + 1) * SHD)
                    q = sqT[r, head // 2, t * P:(t + 1) * P]
                    kt = skT[r, head // (SH // SKV), :]
                    mm = nc.tensor.matmul(raw[n % 2][:, NCTX:2 * NCTX], q, kt[:, 0:NCTX], start=True, stop=True)
                    if near:
                        mm = nc.tensor.matmul(raw[n % 2][:, 512:512 + len(near) * P], q,
                                              kt[:, near[0] * P:(near[-1] + 1) * P], start=True, stop=True)
                    mm.then_inc(scored, 1)

                def turn_quad(n):
                    t, b, q = quads[n]
                    pe.wait_ge(probs, SH * t + 4 * (q + 1))
                    if n >= 2:
                        pe.wait_ge((placed_v, placed_a)[n % 2], n // 2)
                    for i in range(4):
                        mm = nc.tensor.transpose(turn[n % 2][:, i, :], s[t % 2][:, 4 * q + i, b * P:(b + 1) * P],
                                                 tr.ident[:])
                    mm.then_inc(turned, 1)

                def values(t):
                    ks = keys(t)[0]
                    pe.wait_ge(placed_v, before(t + 1) // 2)
                    pe.wait_ge(placed_a, before(t + 1) // 2)
                    if t >= 2:
                        pe.wait_ge(normed, t - 1)
                    for head in range(SH):
                        g = head // (SH // SKV)
                        for b, j in enumerate(ks):
                            mm = nc.tensor.matmul(op[t % 2][:, head, :], pT[:, b, head, :],
                                                  sv[:, j, g * SHD:(g + 1) * SHD],
                                                  start=(b == 0), stop=(b == len(ks) - 1))
                    mm.then_inc(attended, 1)

                for head in range(SH):
                    score(0, head)
                for t in range(NT):
                    for head, quad in steps(t):
                        if head is not None:
                            score(t + 1, head)
                        if quad is not None:
                            turn_quad(quad)
                    values(t)

            @block.vector
            def _(dve):
                dve.wait_ge(loaded, 32)

                def mask_scores(t, head):
                    nk = len(keys(t)[0]) * P
                    n = t * SH + head
                    dve.wait_ge(scored, n + 1)
                    if t >= 2:
                        dve.wait_ge(turned, before(t - 1))
                    nc.vector.tensor_tensor_reduce(s[t % 2][:, head, 0:nk], raw[n % 2][:, NCTX:NCTX + nk],
                                                   mask[:, keys(t)[1], 0:nk], 1.0, NEG, ALU.add, ALU.max,
                                                   top[:, t, head:head + 1]).then_inc(masked, 1)

                def maxima(t):
                    dve.wait_ge(masked, SH * (t + 1))
                    nc.vector.scalar_tensor_tensor(m[:, t, :], top[:, t, :], scale, sink[:], ALU.mult, ALU.max) \
                        .then_inc(maxed, 1)
                    dve.wait_ge(maxed, t + 1)
                    nc.vector.tensor_scalar(nm[:, t, :], m[:, t, :], -1.0, None, ALU.mult).then_inc(negated, 1)
                    nc.vector.tensor_tensor(ed[:, t, :], sink[:], m[:, t, :], ALU.subtract).then_inc(diff, 1)

                def place(n):
                    t, b, q = quads[n]
                    if t >= 1:
                        dve.wait_ge(attended, t)
                    dve.wait_ge(turned, n + 1)
                    nc.vector.tensor_copy(pT[:, b, 4 * q:4 * q + 4, :], turn[0][:]).then_inc(placed_v, 1)

                def norm(t):
                    dve.wait_ge(sinks, t + 1)
                    dve.wait_ge(probs, SH * (t + 1))
                    nc.vector.tensor_tensor(den[:, t, :], total[:, t, :], es[:, t, :], ALU.add).then_inc(summed, 1)
                    dve.wait_ge(summed, t + 1)
                    nc.vector.reciprocal(rden[:, t, :], den[:, t, :]).then_inc(inverted, 1)
                    dve.wait_ge(inverted, t + 1)
                    dve.wait_ge(attended, t + 1)
                    nc.vector.tensor_tensor(cat[:, t, GH * GDV:D].rearrange("p (h e) -> p h e", h=SH), op[t % 2][:],
                                            rden[:, t, :].unsqueeze(2).to_broadcast([P, SH, SHD]), ALU.mult) \
                        .then_inc(normed, 1)

                for head in range(SH):
                    mask_scores(0, head)
                maxima(0)
                for t in range(NT):
                    for head, quad in steps(t):
                        if head is not None:
                            mask_scores(t + 1, head)
                            if head == SH - 1:
                                maxima(t + 1)
                        if quad is not None and quad % 2 == 0:
                            place(quad)
                    norm(t)

            @block.scalar
            def _(act):
                def exps(t):
                    nk = len(keys(t)[0]) * P
                    act.wait_ge(negated, t + 1)
                    for head in range(SH):
                        nc.scalar.activation(s[t % 2][:, head, 0:nk], s[t % 2][:, head, 0:nk], ACT.Exp,
                                             bias=nm[:, t, head:head + 1], scale=scale,
                                             accum_out=total[:, t, head:head + 1]).then_inc(probs, 1)
                    act.wait_ge(diff, t + 1)
                    nc.scalar.activation(es[:, t, :], ed[:, t, :], ACT.Exp).then_inc(sinks, 1)

                def place(t):
                    for n in range(before(t), before(t + 1)):
                        if n % 2 == 1:
                            _, b, q = quads[n]
                            if t >= 1:
                                act.wait_ge(attended, t)
                            act.wait_ge(turned, n + 1)
                            nc.scalar.copy(pT[:, b, 4 * q:4 * q + 4, :], turn[1][:]).then_inc(placed_a, 1)

                exps(0)
                for t in range(NT):
                    place(t)
                    if t + 1 < NT:
                        exps(t + 1)


def even_mixer(tr, layer):
    nc = tr.nc
    with ExitStack() as st:
        def sb(name, shape):
            return st.enter_context(nc.sbuf_tensor(name, shape, F32))

        cat = sb("cat_e", [P, NT, D])
        with ExitStack() as st:
            early = sb("early", [P, 3, NT * GH * GDV])
            qkT = early[:, 0, :].rearrange("p (x t) -> p x t", x=4)
            v, gs = (early[:, i, :].rearrange("p (t n) -> p t n", t=NT) for i in (1, 2))
            w_out = early[:].rearrange("p i n -> p (i n)")[:, 0:KD * D].rearrange("p (k n) -> p k n", k=KD)
            out_loaded = nc.alloc_semaphore("w_out_e_loaded")
            with ExitStack() as st:
                aT, sqT, skT = sb("aT", [2 * GRANK, T]), sb("sqT", [P, SH // 2, T]), sb("skT", [P, SKV, T])
                sv = sb("sv", [P, NT, SKV * SHD])
                with ExitStack() as st:
                    uT, w = sb("uT_e", [P, KD, T]), [sb(f"w_in_e{i}", [P, KD, SK0 - A0]) for i in range(2)]
                    w_loaded = [nc.alloc_semaphore(f"w_in_e_loaded{i}") for i in range(2)]

                    def load_ahead(sp):
                        for g in range(2):
                            load_group(sp, tr, w, w_loaded, g)

                    norm_transpose(tr, layer, uT, load_ahead)
                    even_project(tr, uT, qkT, aT, sqT, skT, v, gs, sv, cat, w, w_loaded)
                with ExitStack() as st:
                    qa, kb = sb("qa", [P, 4, T]), sb("kb", [P, 4, T])
                    carry, sm = sb("carry", [P, 2, NT, 2]), sb("sm", [P, NT, 4, GDV])
                    gla_decays(tr, qkT, aT, qa, kb, carry)
                    gla_states(tr, kb, v, carry, sm)
                    gla_outputs(tr, qa, kb, v, sm, gs, cat)
                rotate(tr, [sqT[:, i, NCTX:T] for i in range(SH // 2)] + [skT[:, i, NCTX:T] for i in range(SKV)])
                window_attention(tr, sqT, skT, sv, cat, lambda sp: sp.dma_start(
                    w_out, tr.dram["w_out_e"][0].rearrange("(p k) n -> p k n", k=KD)).then_inc(out_loaded, 16))
            mix_and_route(tr, layer, cat, list(range(NT)), w_out, out_loaded)
        experts_and_sum(tr, layer, cat, list(range(NT)))


def mod_vector(tr, layer, i, s):
    return tr.mod_row[layer, i, s:s + 1, :].to_broadcast([P, D])


def mix_out(tr, layer, cat, vT, tiles, w, w_loaded):
    nc = tr.nc
    n_t = len(tiles)
    kinds = [0, 1] if tiles[0] < CT else [0]
    with Phase(nc) as ph:
        ph.adopt([w_loaded])
        mb = ph.sb("mod_b", [P, 3, len(kinds), D])
        cT = [ph.sb(f"cT{i}", [P, KD, P]) for i in range(2)]
        tmp = [ph.sb(f"tmp{i}", [P, D]) for i in range(2)]
        row = [ph.sb(f"row{i}", [P, D]) for i in range(2)]
        sq = ph.sb("sq", [P, D])
        ss, rt, rs = ph.sb("ss", [P, 2, n_t]), ph.sb("rt", [P, 2, n_t]), ph.sb("rs", [P, 2, n_t])
        cb = [ph.ps(f"cb{i}", [P, 4, P]) for i in range(2)]
        yb = [ph.ps(f"yb{i}", [P, D]) for i in range(2)]
        vb = [ph.ps(f"vb{i}", [P, 4, P]) for i in range(2)]
        loaded = ph.sem("vectors_loaded")
        cat_turned, cat_v, cat_a = ph.sem("cat_turned"), ph.sem("cat_placed_v"), ph.sem("cat_placed_a")
        y_done, squared, rooted, inverted = ph.sem("y_done"), ph.sem("squared"), ph.sem("rooted"), ph.sem("inverted")
        y_scaled, h_done, scaled, row_done = ph.sem("y_scaled"), ph.sem("h_done"), ph.sem("scaled"), ph.sem("row_done")
        row_stored = [ph.sem(f"row_stored{i}") for i in range(2)]
        v_turned, v_v, v_a = ph.sem("v_turned"), ph.sem("v_placed_v"), ph.sem("v_placed_a")
        with ph.block() as block:
            @block.sync
            def _(sp):
                for i in range(3):
                    for s in kinds:
                        sp.dma_start(mb[:, i, s, :], mod_vector(tr, layer, i, s)).then_inc(loaded, 16)
                for n, t in enumerate(tiles):
                    sp.wait_ge(row_done, n + 1)
                    sp.dma_start(tr.rows_x[t * P:(t + 1) * P, :], row[n % 2][:]).then_inc(row_stored[n % 2], 16)
                sp.wait_ge(row_stored[0], 16 * ((n_t + 1) // 2))
                sp.wait_ge(row_stored[1], 16 * (n_t // 2))

            @block.tensor
            def _(pe):
                def turn_cat(n):
                    for half in range(2):
                        if n:
                            pe.wait_ge(cat_a if half else cat_v, n)
                        for k in range(4):
                            mm = nc.tensor.transpose(cb[half][:, k, :], cat[:, tiles[n], half * 4 + k:D:KD], tr.ident[:])
                        mm.then_inc(cat_turned, 1)

                def turn_v(n):
                    pe.wait_ge(row_done, n + 1)
                    for half in range(2):
                        if n:
                            pe.wait_ge(v_a if half else v_v, n)
                        for k in range(4):
                            mm = nc.tensor.transpose(vb[half][:, k, :], row[n % 2][:, half * 4 + k:D:KD], tr.ident[:])
                        mm.then_inc(v_turned, 1)

                turn_cat(0)
                pe.wait_ge(w_loaded, 16)
                for n in range(n_t):
                    if n + 1 < n_t:
                        turn_cat(n + 1)
                    pe.wait_ge(cat_v, n + 1)
                    pe.wait_ge(cat_a, n + 1)
                    if n >= 2:
                        pe.wait_ge(y_scaled, n - 1)
                    for half in range(2):
                        for k in range(KD):
                            mm = nc.tensor.matmul(yb[n % 2][:, half * 512:(half + 1) * 512], cT[n % 2][:, k, :],
                                                  w[:, k, half * 512:(half + 1) * 512],
                                                  start=(k == 0), stop=(k == KD - 1))
                    mm.then_inc(y_done, 1)
                    if n:
                        turn_v(n - 1)
                turn_v(n_t - 1)

            @block.scalar
            def _(act):
                def place_cat(n):
                    act.wait_ge(cat_turned, 2 * n + 2)
                    if n >= 2:
                        act.wait_ge(y_done, n - 1)
                    nc.scalar.copy(cT[n % 2][:, 4:8, :], cb[1][:]).then_inc(cat_a, 1)

                def root(n, which, src):
                    if 2 * n + which:
                        act.wait_ge(squared, 2 * n + which)
                    nc.scalar.activation(sq[:], src, ACT.Square, accum_out=ss[:, which, n:n + 1]).then_inc(squared, 1)
                    act.wait_ge(squared, 2 * n + which + 1)
                    nc.scalar.activation(rt[:, which, n:n + 1], ss[:, which, n:n + 1], ACT.Sqrt,
                                         bias=tr.eps[:, 0:1], scale=1.0 / D).then_inc(rooted, 1)

                def place_v(n):
                    act.wait_ge(v_turned, 2 * n + 2)
                    nc.scalar.copy(vT[:, 4:8, tiles[n] * P:(tiles[n] + 1) * P], vb[1][:]).then_inc(v_a, 1)

                place_cat(0)
                for n, t in enumerate(tiles):
                    if n + 1 < n_t:
                        place_cat(n + 1)
                    act.wait_ge(y_done, n + 1)
                    root(n, 0, yb[n % 2][:])
                    act.wait_ge(h_done, n + 1)
                    root(n, 1, tr.h[:, t, :])
                    if n:
                        place_v(n - 1)
                place_v(n_t - 1)

            @block.vector
            def _(dve):
                def place_cat(n):
                    dve.wait_ge(cat_turned, 2 * n + 1)
                    if n >= 2:
                        dve.wait_ge(y_done, n - 1)
                    nc.vector.tensor_copy(cT[n % 2][:, 0:4, :], cb[0][:]).then_inc(cat_v, 1)

                def place_v(n):
                    dve.wait_ge(v_turned, 2 * n + 1)
                    nc.vector.tensor_copy(vT[:, 0:4, tiles[n] * P:(tiles[n] + 1) * P], vb[0][:]).then_inc(v_v, 1)

                def invert(n, which):
                    dve.wait_ge(rooted, 2 * n + which + 1)
                    nc.vector.reciprocal(rs[:, which, n:n + 1], rt[:, which, n:n + 1]).then_inc(inverted, 1)
                    dve.wait_ge(inverted, 2 * n + which + 1)

                place_cat(0)
                dve.wait_ge(loaded, 16 * 3 * len(kinds))
                for n, t in enumerate(tiles):
                    s = 1 if t < CT else 0
                    if n + 1 < n_t:
                        place_cat(n + 1)
                    invert(n, 0)
                    if n >= 2:
                        dve.wait_ge(row_done, n - 1)
                    nc.vector.scalar_tensor_tensor(tmp[n % 2][:], yb[n % 2][:], rs[:, 0, n:n + 1], mb[:, 0, s, :],
                                                   ALU.mult, ALU.mult).then_inc(y_scaled, 1)
                    dve.wait_ge(y_scaled, n + 1)
                    nc.vector.tensor_tensor(tr.h[:, t, :], tr.h[:, t, :], tmp[n % 2][:], ALU.add).then_inc(h_done, 1)
                    dve.wait_ge(h_done, n + 1)
                    invert(n, 1)
                    nc.vector.scalar_tensor_tensor(tmp[n % 2][:], tr.h[:, t, :], rs[:, 1, n:n + 1], mb[:, 1, s, :],
                                                   ALU.mult, ALU.mult).then_inc(scaled, 1)
                    if n:
                        place_v(n - 1)
                place_v(n_t - 1)

            @block.gpsimd
            def _(pool):
                pool.wait_ge(loaded, 16 * 3 * len(kinds))
                for n, t in enumerate(tiles):
                    s = 1 if t < CT else 0
                    pool.wait_ge(scaled, n + 1)
                    if n >= 2:
                        pool.wait_ge(row_stored[n % 2], 16 * (n // 2))
                        pool.wait_ge(v_turned, 2 * (n - 1))
                    nc.gpsimd.tensor_tensor(row[n % 2][:], tmp[n % 2][:], mb[:, 2, s, :], ALU.add).then_inc(row_done, 1)


BEND = SLOTB // 2
PAIRS_AT, LAST_AT, STORED_AT, LAST_BUT_ONE_AT = BEND + NE, BEND + NE + 1, BEND + NE + 2, BEND + NE + 3
TABLE = LAST_BUT_ONE_AT + 1


def route(tr, layer, vT, f, tiles):
    nc, dr = tr.nc, tr.dram
    n_t = len(tiles)
    POOL_MULTS = 2
    with Phase(nc) as ph:
        wg = ph.sb("wg", [P, KD, 2, DE])
        wd = ph.sb("wd", [P, 2, D])
        wr = ph.sb("wr", [P, KD, NE])
        bias = ph.sb("bias", [P, NE])
        before, name = ph.sb("before", [P, P]), ph.sb("name", [P, NT, TOPK])
        A = [P, n_t, NE]
        score, sel, chosen, weight, dest = (ph.sb(x, A) for x in ("score", "sel", "chosen", "weight", "dest"))
        m8 = ph.sb("m8", [P, n_t, NG, 8])
        grp, grp2, top4 = ph.sb("grp", [P, n_t, 12]), ph.sb("grp2", [P, n_t, 12]), ph.sb("top4", [P, n_t, 8])
        g8, pen = ph.sb("g8", [P, n_t, 8]), ph.sb("pen", [P, n_t, NG])
        top, d8 = ph.sb("top", [P, n_t, 8]), ph.sb("d8", [P, n_t, 8])
        wsum, wrec = ph.sb("wsum", [P, n_t]), ph.sb("wrec", [P, n_t])
        junk = ph.sb("junk", [P, n_t, 8, NE])
        nb, bend, base, one64 = (ph.sb(x, [P, NE]) for x in ("nb", "bend", "base", "one64"))
        eo, eom = ph.sb("eo", [P, 1]), ph.sb("eom", [P, 1])
        eb, word = ph.sb("eb", [1, SLOTB]), ph.sb("word", [1, SLOTB // 2 - 1])
        eoj, pair = ph.sb("eoj", [P, NE]), ph.sb("pair", [1, 2], I32)
        slots, slots4 = ph.sb("slots", [SLOTB, P]), ph.sb("slots4", [SLOTB, QUADS, QUADS, P // QUADS])
        quad, row_of, token = ph.sb("quad", [P, 1]), ph.sb("row_of", [P, 1]), ph.sb("token", [SLOTB, P], I32)
        sg, up = [ph.sb(f"sg{i}", [P, DE]) for i in range(2)], [ph.sb(f"up{i}", [P, DE]) for i in range(2)]
        hid, hT = [ph.sb(f"hid{i}", [P, DE]) for i in range(2)], [ph.sb(f"hT{i}", [P, 2, P]) for i in range(2)]
        HALF = n_t * P // 2
        lT, by_expert, lT_read = ph.sb("lT", [NE, n_t * P]), ph.sem("logits_by_expert"), ph.sem("logits_read")
        lg = ph.ps("lg", [P, n_t, NE])
        pairs_t, pairs_turned = lg[:].rearrange("p n e -> p (n e)")[:, 0:SLOTB], ph.sem("pairs_turned")
        rank = ph.ps("rank", [P, n_t + 1, NE])
        gu = [ph.ps(f"gu{i}", [P, 512]) for i in range(2)]
        hb = ph.ps("hb", [P, 2, P])
        yb = ph.ps("yb", [P, D])
        tab = ph.ps("tab", [P, QUADS, P])
        loaded, sh_loaded = ph.sem("router_loaded"), ph.sem("shared_loaded")
        logits, scored, step, picked = ph.sem("logits"), ph.sem("scored"), ph.sem("route_step"), ph.sem("picked")
        ranked, dest_done, ends_done = ph.sem("ranked"), ph.sem("dest_done"), ph.sem("ends_done")
        scattered, slots_loaded = ph.sem("scattered"), ph.sem("slots_loaded")
        eo_row, slots_turned, repeated = ph.sem("eo_row"), ph.sem("slots_turned"), ph.sem("slots_repeated")
        gu_done, gu_read, hid_pool, hid_dve = ph.sem("gu_done"), ph.sem("gu_read"), ph.sem("hid_pool"), ph.sem("hid_dve")
        h_turned, h_placed, y_done, y_read = ph.sem("h_turned"), ph.sem("h_placed"), ph.sem("y_done"), ph.sem("y_read")

        def wait_hid(eng, n):
            if n < POOL_MULTS:
                eng.wait_ge(hid_pool, n + 1)
            else:
                eng.wait_ge(hid_dve, n + 1 - POOL_MULTS)

        with ph.block() as block:
            @block.sync
            def _(sp):
                sp.dma_start(wr[:], dr["w_router"][layer].rearrange("(p k) e -> p k e", k=KD)).then_inc(loaded, 16)
                sp.dma_start(bias[:], dr["b_router"][layer:layer + 1].to_broadcast([P, NE])).then_inc(loaded, 16)
                sp.dma_start(before[:], dr["c_before"]).then_inc(loaded, 16)
                sp.dma_start(name[:], dr["c_name"]).then_inc(loaded, 16)
                sp.dma_start(quad[:], dr["c_quad"]).then_inc(loaded, 16)
                sp.dma_start(row_of[:], dr["c_row"]).then_inc(loaded, 16)
                for i, n in enumerate(("w_sh_gate", "w_sh_up")):
                    sp.dma_start(wg[:, :, i, :], dr[n][layer].rearrange("(p k) n -> p k n", k=KD)) \
                        .then_inc(sh_loaded, 16)
                sp.dma_start(wd[:], dr["w_sh_down"][layer].rearrange("(p k) n -> p k n", k=2)).then_inc(sh_loaded, 16)
                sp.wait_ge(scattered, 16 * n_t * TOPK)
                sp.dma_start(slots[:], tr.slot_name[layer].rearrange("(g r) o -> g (r o)", g=SLOTB)) \
                    .then_inc(slots_loaded, 16)

            @block.tensor
            def _(pe):
                pe.wait_ge(loaded, 96)
                for hf in range(2):
                    lo = tiles[0] * P + hf * HALF
                    for k in range(KD):
                        mm = nc.tensor.matmul(gu[hf][0:NE, 0:HALF], wr[:, k, :], vT[:, k, lo:lo + HALF],
                                              start=(k == 0), stop=(k == KD - 1))
                    mm.then_inc(by_expert, 1)
                for n in range(n_t):
                    pe.wait_ge(lT_read, (n * P) // HALF + 1)
                    mm = nc.tensor.transpose(lg[:, n, :], lT[:, n * P:(n + 1) * P], tr.ident[0:NE, 0:NE])
                mm.then_inc(logits, 1)

                def gate_up(n):
                    t = tiles[n]
                    if n >= 2:
                        wait_hid(pe, n - 2)
                        pe.wait_ge(gu_read, n - 1)
                    for k in range(KD):
                        mm = nc.tensor.matmul(gu[n % 2][:], vT[:, k, t * P:(t + 1) * P],
                                              wg[:, k, :, :].rearrange("p a b -> p (a b)"),
                                              start=(k == 0), stop=(k == KD - 1))
                    mm.then_inc(gu_done, 1)

                def turn_hidden(n):
                    wait_hid(pe, n)
                    if n:
                        pe.wait_ge(h_placed, n)
                    for k in range(2):
                        mm = nc.tensor.transpose(hb[:, k, :], hid[n % 2][:, k:DE:2], tr.ident[:])
                    mm.then_inc(h_turned, 1)

                def down(n):
                    pe.wait_ge(h_placed, n + 1)
                    if n:
                        pe.wait_ge(y_read, n)
                    for half in range(2):
                        for k in range(2):
                            mm = nc.tensor.matmul(yb[:, half * 512:(half + 1) * 512], hT[n % 2][:, k, :],
                                                  wd[:, k, half * 512:(half + 1) * 512],
                                                  start=(k == 0), stop=(k == 1))
                    mm.then_inc(y_done, 1)

                def ranks():
                    pe.wait_ge(picked, 1)
                    for n in range(n_t):
                        for m in range(n + 1):
                            nc.tensor.matmul(rank[:, n, :], before[:] if m == n else tr.ones[:], chosen[:, m, :],
                                             start=(m == 0), stop=(m == n))
                    for m in range(n_t):
                        mm = nc.tensor.matmul(rank[:, n_t, :], tr.ones[:], chosen[:, m, :],
                                              start=(m == 0), stop=(m == n_t - 1))
                    mm.then_inc(ranked, 1)

                pe.wait_ge(sh_loaded, 48)
                for n in range(n_t):
                    gate_up(n)
                    if n:
                        down(n - 1)
                    turn_hidden(n)
                    if n == 0:
                        ranks()
                down(n_t - 1)
                pe.wait_ge(ends_done, 1)
                nc.tensor.matmul(tab[0:1, 0, :], eom[:], tr.ident[:], start=True, stop=True).then_inc(eo_row, 1)
                pe.wait_ge(slots_loaded, 16)
                nc.tensor.transpose(pairs_t, slots[:], tr.ident[:]).then_inc(pairs_turned, 1)
                pe.wait_ge(repeated, 1)
                pe.wait_ge(ends_done, 2)
                for q in range(QUADS):
                    mm = nc.tensor.transpose(tab[:, q, :], slots4[:, q].rearrange("g a b -> g (a b)"), tr.ident[:])
                mm.then_inc(slots_turned, 1)

            @block.scalar
            def _(act):
                act.wait_ge(logits, 1)
                nc.scalar.activation(score[:], lg[:], ACT.Sigmoid).then_inc(scored, 1)

                def read_gate_up(n):
                    act.wait_ge(gu_done, n + 1)
                    if n >= 2:
                        wait_hid(act, n - 2)
                    nc.scalar.activation(sg[n % 2][:], gu[n % 2][:, 0:DE], ACT.Silu)
                    nc.scalar.copy(up[n % 2][:], gu[n % 2][:, DE:2 * DE]).then_inc(gu_read, 1)

                read_gate_up(0)
                for n in range(n_t):
                    act.wait_ge(h_turned, n + 1)
                    if n >= 2:
                        act.wait_ge(y_done, n - 1)
                    nc.scalar.copy(hT[n % 2][:], hb[:]).then_inc(h_placed, 1)
                    if n + 1 < n_t:
                        read_gate_up(n + 1)
                    act.wait_ge(y_done, n + 1)
                    nc.scalar.copy(f[:, tiles[n], :], yb[:]).then_inc(y_read, 1)

            @block.gpsimd
            def _(pool):
                for n in range(POOL_MULTS):
                    pool.wait_ge(gu_read, n + 1)
                    nc.gpsimd.tensor_tensor(hid[n % 2][:], sg[n % 2][:], up[n % 2][:], ALU.mult).then_inc(hid_pool, 1)
                pool.wait_ge(dest_done, 1)
                for n, t in enumerate(tiles):
                    for k in range(TOPK):
                        nc.gpsimd.indirect_dma_start(
                            out=tr.slot_name[layer][:, :],
                            out_offset=bass.IndirectOffsetOnAxis(ap=tr.dest8[:, n, k:k + 1], axis=0),
                            in_=name[:, t, k:k + 1], in_offset=None).then_inc(scattered, 16)
                pool.wait_ge(scattered, 16 * n_t * TOPK)

            @block.vector
            def _(dve):
                order = [0]

                def link(ins):
                    order[0] += 1
                    ins.then_inc(step, 1)
                    dve.wait_ge(step, order[0])

                nc.vector.memset(one64[:], 1.0)
                nc.vector.memset(grp[:, :, NG:12], NEG)
                link(nc.vector.memset(top4[:, :, TG:8], NEG))
                for hf in range(2):
                    dve.wait_ge(by_expert, hf + 1)
                    nc.vector.tensor_copy(lT[:, hf * HALF:(hf + 1) * HALF], gu[hf][0:NE, 0:HALF]).then_inc(lT_read, 1)
                dve.wait_ge(loaded, 96)
                dve.wait_ge(scored, 1)
                link(nc.vector.tensor_tensor(sel[:], score[:], bias[:].unsqueeze(1).to_broadcast(A), ALU.add))
                for n in range(n_t):
                    for g in range(NG):
                        ins = nc.vector.max(m8[:, n, g, :], sel[:, n, g * EG:(g + 1) * EG])
                link(ins)
                link(nc.vector.tensor_tensor(grp[:, :, 0:NG], m8[:, :, :, 0], m8[:, :, :, 1], ALU.add))
                for n in range(n_t):
                    ins = nc.vector.max(g8[:, n, :], grp[:, n, 0:NG])
                link(ins)
                link(nc.vector.tensor_copy(top4[:, :, 0:TG], g8[:, :, 0:TG]))
                for n in range(n_t):
                    ins = nc.vector.match_replace(grp2[:, n, :], top4[:, n, :], grp[:, n, :], 2 * NEG)
                link(ins)
                link(nc.vector.tensor_scalar(pen[:], grp2[:, :, 0:NG], 2 * NEG, 1.0, ALU.is_equal, ALU.subtract))
                for n in range(n_t):
                    ins = nc.vector.scalar_tensor_tensor(
                        sel[:, n, :].rearrange("p (g e) -> p g e", g=NG),
                        pen[:, n, :].unsqueeze(2).to_broadcast([P, NG, EG]), -NEG,
                        sel[:, n, :].rearrange("p (g e) -> p g e", g=NG), ALU.mult, ALU.add)
                link(ins)
                for n in range(n_t):
                    ins = nc.vector.max(top[:, n, :], sel[:, n, :])
                link(ins)
                for n in range(n_t):
                    ins = nc.vector.match_replace(dest[:, n, :], top[:, n, :], sel[:, n, :], 2 * NEG)
                link(ins)
                nc.vector.tensor_scalar(chosen[:], dest[:], 2 * NEG, None, ALU.is_equal).then_inc(picked, 1)
                dve.wait_ge(picked, 1)
                link(nc.vector.tensor_tensor(weight[:], score[:], chosen[:], ALU.mult))
                link(nc.vector.reduce_sum(wsum[:], weight[:], AX))
                link(nc.vector.reciprocal(wrec[:], wsum[:]))
                for n in range(n_t):
                    ins = nc.vector.tensor_scalar(weight[:, n, :], weight[:, n, :], wrec[:, n:n + 1], ROUTED,
                                                  ALU.mult, ALU.mult)
                link(ins)
                dve.wait_ge(ranked, 1)
                total = rank[:, n_t, :]
                link(nc.vector.tensor_scalar(nb[:], total, float(P), 1.0, ALU.is_gt, ALU.add))
                for b in range(2, n_t):
                    link(nc.vector.scalar_tensor_tensor(nb[:], total, float(b * P), nb[:], ALU.is_gt, ALU.add))
                link(nc.vector.tensor_tensor_scan(bend[:], one64[:], nb[:], 0.0, ALU.mult, ALU.add))
                link(nc.vector.tensor_tensor(base[:], bend[:], nb[:], ALU.subtract))
                link(nc.vector.tensor_scalar(base[:], base[:], float(P), 1.0, ALU.mult, ALU.add))
                link(nc.vector.tensor_tensor(dest[:], rank[:, 0:n_t, :], base[:].unsqueeze(1).to_broadcast(A), ALU.add))
                link(nc.vector.tensor_tensor(dest[:], dest[:], chosen[:], ALU.mult))
                for n in range(n_t):
                    ins = nc.vector.max(d8[:, n, :], dest[:, n, :])
                link(ins)
                nc.vector.tensor_scalar(tr.dest8[:, 0:n_t, :], d8[:], -1.0, None, ALU.add).then_inc(dest_done, 1)
                link(nc.vector.tensor_scalar(eoj[:], bend[:], row_of[:, 0:1], 0.0, ALU.is_le, ALU.add, accum_out=eo[:]))
                nc.vector.tensor_scalar(eom[:], eo[:], float(NE - 1), None, ALU.min).then_inc(ends_done, 1)
                nc.vector.tensor_copy(tr.blocks[0:1, BEND:BEND + NE], bend[0:1, :])
                link(nc.vector.tensor_scalar(pair[:, 0:1], bend[0:1, NE - 1:NE], 1.0, None, ALU.add))
                link(nc.vector.tensor_scalar(pair[:, 1:2], pair[:, 0:1], 1, None, ALU.logical_shift_right))
                nc.vector.tensor_copy(tr.blocks[0:1, PAIRS_AT:PAIRS_AT + 1], pair[:, 1:2])
                nc.vector.tensor_scalar(tr.blocks[0:1, LAST_AT:LAST_AT + 1], pair[:, 1:2], 2.0, -1.0,
                                        ALU.mult, ALU.add)
                nc.vector.tensor_scalar(tr.blocks[0:1, LAST_BUT_ONE_AT:LAST_BUT_ONE_AT + 1], pair[:, 1:2], 2.0, -2.0,
                                        ALU.mult, ALU.add)
                nc.vector.tensor_scalar(tr.blocks[0:1, STORED_AT:STORED_AT + 1], pair[:, 1:2], 16.0, -16.0,
                                        ALU.mult, ALU.add)
                for n in range(n_t):
                    for k in range(TOPK):
                        nc.vector.scalar_tensor_tensor(junk[:, n, k, :], dest[:, n, :], d8[:, n, k:k + 1],
                                                       weight[:, n, :], ALU.is_equal, ALU.mult,
                                                       accum_out=tr.w8[:, n, k:k + 1])
                for n in range(POOL_MULTS, n_t):
                    dve.wait_ge(gu_read, n + 1)
                    if n >= 2:
                        dve.wait_ge(h_turned, n - 1)
                    nc.vector.tensor_tensor(hid[n % 2][:], sg[n % 2][:], up[n % 2][:], ALU.mult).then_inc(hid_dve, 1)
                dve.wait_ge(eo_row, 1)
                link(nc.vector.tensor_copy(eb[:], tab[0:1, 0, :]))
                link(nc.vector.scalar_tensor_tensor(word[:], eb[:, 1:SLOTB - 2:2], float(NE), eb[:, 2:SLOTB - 1:2],
                                                    ALU.mult, ALU.add))
                nc.vector.scalar_tensor_tensor(tr.blocks[0:1, 1:SLOTB // 2], word[:], float(NE), eb[:, 3:SLOTB:2],
                                               ALU.mult, ALU.add).then_inc(ends_done, 1)
                dve.wait_ge(slots_loaded, 16)
                link(nc.vector.tensor_copy(token[:], slots[:]))
                link(nc.vector.tensor_scalar(token[:], token[:], TOPK.bit_length() - 1, None,
                                             ALU.logical_shift_right))
                nc.vector.tensor_copy(slots4[:], token[:].rearrange("g (q b) -> g q b", q=QUADS).unsqueeze(2)
                                      .to_broadcast([SLOTB, QUADS, QUADS, P // QUADS])).then_inc(repeated, 1)
                dve.wait_ge(slots_turned, 1)
                nc.vector.tensor_scalar(tr.slot_row[:], tab[:], float(QUADS), quad[:, 0:1], ALU.mult, ALU.add)
                dve.wait_ge(pairs_turned, 1)
                nc.vector.tensor_copy(tr.slot_pair[:], pairs_t)


def experts(tr, layer):
    nc, dr = tr.nc, tr.dram
    PAIRS = MAXBLK // 2
    W = 2 * KD * DE + 2 * D
    with Phase(nc) as ph:
        ring = ph.sb("ring", [P, LOADED, W])
        xg = [ph.sb(f"xg{i}", [P, D]) for i in range(2)]
        y_idx = [ph.sb(f"y_idx{i}", [P, 1], I32) for i in range(2)]
        idx = [ph.sb(f"idx{i}", [P, QUADS], I32) for i in range(2)]
        xT = [ph.sb(f"xT{i}", [P, KD, P]) for i in range(2)]
        sg, hid = [ph.sb(f"sg{i}", [P, DE]) for i in range(2)], [ph.sb(f"hid{i}", [P, DE]) for i in range(2)]
        hT = [ph.sb(f"hT{i}", [P, 2, P]) for i in range(2)]
        ys = [ph.sb(f"ys{i}", [P, D]) for i in range(2)]
        gu = [ph.ps(f"gu{i}", [P, 512]) for i in range(2)]
        hb = ph.ps("hb", [P, 2, P])
        yb = [ph.ps(f"yb{i}", [P, 512]) for i in range(2)]
        landed = [ph.sem(f"weights_landed{i}") for i in range(LOADED)]
        weights_ready, y_done = ph.sem("weights_ready"), ph.sem("y_done")
        copied, gathered = ph.sem("index_copied"), [ph.sem(f"gathered{i}") for i in range(2)]
        cleared, x_turned = ph.sem("cleared"), ph.sem("x_turned")
        gu_done, silu_done, hid_ready = ph.sem("gate_up_done"), ph.sem("silu_done"), ph.sem("hidden_ready")
        h_turned, h_placed = ph.sem("h_turned"), ph.sem("h_placed")
        y_v, y_a = ph.sem("y_read_v"), ph.sem("y_read_a")
        stored = [ph.sem(f"stored{i}") for i in range(2)]

        seen, all_stored = ph.sem("index_seen"), ph.sem("all_stored")
        y_copied, y_seen = ph.sem("y_index_copied"), ph.sem("y_seen")

        def table(eng, at, low, high):
            return eng.value_load(tr.blocks[0:1, at:at + 1], min_val=low, max_val=high)

        def pair_count(eng):
            return table(eng, PAIRS_AT, NE // 2, PAIRS)

        def each_pair(eng, pairs, first, groups, body):
            size = (PAIRS - first) // groups
            with eng.Fori(0, groups) as o:
                with eng.If(o * size + first < pairs):
                    with eng.Fori(0, size) as j:
                        i = o * size + j + first
                        with eng.If(i < pairs):
                            body(i)

        def last_block(eng):
            return table(eng, LAST_AT, NE - 1, MAXBLK - 1)

        with ph.block() as block:
            @block.sync
            def _(sp):
                def load(e, slot):
                    dst = ring[:, slot, :]
                    for i, name in enumerate(("w_exp_gate", "w_exp_up")):
                        w_dram = dr[name][layer].rearrange("e (p k) n -> p e k n", k=KD)
                        d = dst[:, 0:2 * KD * DE].rearrange("p (i k n) -> p i k n", i=2, k=KD)[:, i]
                        sp.dma_start(d, w_dram[:, bass.ds(e, 1)].rearrange("p e k n -> p (e k) n")) \
                            .then_inc(landed[slot], 16)
                    w_dram = dr["w_exp_down"][layer].rearrange("e (p k) n -> p e (k n)", k=2)
                    sp.dma_start(dst[:, 2 * KD * DE:W], w_dram[:, bass.ds(e, 1)].rearrange("p e n -> p (e n)")) \
                        .then_inc(landed[slot], 16)

                for e in range(LOADED):
                    if e == 1:
                        sp.wait_ge(seen, 2)
                    load(e, e)
                    if e:
                        sp.wait_ge(landed[e - 1], 48)
                        sp.sem_inc(weights_ready, 1)
                with sp.Fori(1, NE // LOADED) as j:
                    for u in range(LOADED):
                        end = sp.value_load(tr.blocks[0:1, bass.ds(BEND + j * LOADED + (u - LOADED), 1)],
                                            min_val=1, max_val=MAXBLK)
                        sp.wait_ge(y_done, end)
                        load(j * LOADED + u, u)
                        if u:
                            sp.wait_ge(landed[u - 1], j * 48 + 48)
                        else:
                            sp.wait_ge(landed[LOADED - 1], j * 48)
                        sp.sem_inc(weights_ready, 1)
                sp.wait_ge(landed[LOADED - 1], 48 * (NE // LOADED))
                sp.sem_inc(weights_ready, 1)

            @block.gpsimd
            def _(pool):
                def gather(g, q, i, first):
                    if not first:
                        pool.wait_ge(gathered[q], i * 16 * QUADS)
                        pool.wait_ge(x_turned, g - 1)
                    nc.gpsimd.tensor_copy(idx[q][:], tr.slot_row[:, :, bass.ds(g, 1)].rearrange("p q g -> p (q g)")) \
                        .then_inc(copied, 1)
                    pool.wait_ge(copied, g + 1)
                    pool.sem_inc(seen, 1)
                    for part in range(QUADS):
                        nc.gpsimd.indirect_dma_start(
                            out=xg[q][:, part * D // QUADS:(part + 1) * D // QUADS], out_offset=None,
                            in_=tr.rows_x[:, :].rearrange("t (a n) -> (t a) n", a=QUADS),
                            in_offset=bass.IndirectOffsetOnAxis(ap=idx[q][:, part:part + 1], axis=0),
                            bounds_check=QUADS * T - 1, oob_is_err=False).then_inc(gathered[q], 16)

                def store(g, count, q):
                    pool.wait_ge(y_v, count)
                    pool.wait_ge(y_a, count)
                    nc.gpsimd.tensor_copy(y_idx[q][:], tr.slot_pair[:, bass.ds(g, 1)]).then_inc(y_copied, 1)
                    pool.wait_ge(y_copied, count)
                    pool.sem_inc(y_seen, 1)
                    nc.gpsimd.indirect_dma_start(
                        out=tr.rows_y[:, :], out_offset=bass.IndirectOffsetOnAxis(ap=y_idx[q][:, 0:1], axis=0),
                        in_=ys[q][:], in_offset=None, bounds_check=T * TOPK - 1, oob_is_err=False) \
                        .then_inc(stored[q], 16)

                pairs = pair_count(pool)
                for q in range(2):
                    nc.gpsimd.memset(xg[q][:], 0.0).then_inc(cleared, 1)
                pool.wait_ge(cleared, 2)
                gather(0, 0, 0, True)
                gather(1, 1, 0, True)
                gather(2, 0, 1, False)
                gather(3, 1, 1, False)
                gather(4, 0, 2, False)
                store(0, 1, 0)

                def pair_of(i):
                    gather(i * 2 + 1, 1, i, False)
                    store(i * 2 - 3, i * 2 - 2, 1)
                    gather(i * 2 + 2, 0, i + 1, False)
                    store(i * 2 - 2, i * 2 - 1, 0)

                each_pair(pool, pairs, 2, 6, pair_of)
                g = table(pool, LAST_BUT_ONE_AT, NE - 2, MAXBLK - 2)
                store(g - 1, g, 1)
                store(g, g + 1, 0)
                store(g + 1, g + 2, 1)
                before = table(pool, STORED_AT, 16, 16 * PAIRS)
                for q in range(2):
                    pool.wait_ge(stored[q], before + 16)
                    pool.sem_inc(all_stored, 1)

            @block.tensor
            def _(pe):
                def gate_up(q, g, e):
                    pe.wait_ge(weights_ready, e + 1)
                    pe.wait_ge(x_turned, g + 1)
                    slot = e % LOADED
                    wt = ring[:, bass.ds(slot, 1), 0:2 * KD * DE].rearrange("p s (i k n) -> p (s i) k n", i=2, k=KD)
                    for k in range(KD):
                        mm = nc.tensor.matmul(gu[q][:], xT[q][:, k, :], wt[:, :, k, :],
                                              start=(k == 0), stop=(k == KD - 1))
                    mm.then_inc(gu_done, 1)

                def down(q, g, slot, read):
                    pe.wait_ge(h_placed, g + 1)
                    if read:
                        pe.wait_ge(y_v, g)
                        pe.wait_ge(y_a, g)
                    wt = ring[:, bass.ds(slot, 1), 2 * KD * DE:W].rearrange("p s (k n) -> p (s k) n", k=2)
                    for half in range(2):
                        for k in range(2):
                            mm = nc.tensor.matmul(yb[half][:], hT[q][:, k, :], wt[:, k, half * 512:(half + 1) * 512],
                                                  start=(k == 0), stop=(k == 1))
                    mm.then_inc(y_done, 1)

                def turn_hidden(q, g):
                    pe.wait_ge(hid_ready, g + 1)
                    for k in range(2):
                        mm = nc.tensor.transpose(hb[:, k, :], hid[q][:, k:DE:2], tr.ident[:])
                    mm.then_inc(h_turned, 1)

                def experts_of(i):
                    word = pe.value_load(tr.blocks[0:1, bass.ds(i, 1)], min_val=0, max_val=NE ** 3 - 1)
                    return word // NE ** 2, word // NE % NE, word % NE

                pairs = pair_count(pe)
                e1, _, _ = experts_of(1)
                gate_up(0, 0, 0)
                turn_hidden(0, 0)
                gate_up(1, 1, e1)
                down(0, 0, 0, False)
                turn_hidden(1, 1)

                def pair_of(i):
                    e_before, e_a, e_b = experts_of(i)
                    gate_up(0, i * 2, e_a)
                    down(1, i * 2 - 1, e_before % LOADED, True)
                    turn_hidden(0, i * 2)
                    gate_up(1, i * 2 + 1, e_b)
                    down(0, i * 2, e_a % LOADED, True)
                    turn_hidden(1, i * 2 + 1)

                each_pair(pe, pairs, 1, 5, pair_of)
                down(1, last_block(pe), (NE - 1) % LOADED, True)

            @block.scalar
            def _(act):
                def silu(q, g):
                    act.wait_ge(gu_done, g + 1)
                    nc.scalar.activation(sg[q][:], gu[q][:, 0:DE], ACT.Silu).then_inc(silu_done, 1)

                def read_y(q, g, n16):
                    act.wait_ge(y_done, g + 1)
                    if n16 is not None:
                        act.wait_ge(stored[q], n16)
                    nc.scalar.copy(ys[q][:, 512:D], yb[1][:]).then_inc(y_a, 1)

                pairs = pair_count(act)
                silu(0, 0)
                silu(1, 1)
                read_y(0, 0, None)

                def pair_of(i, n16):
                    silu(0, i * 2)
                    read_y(1, i * 2 - 1, n16)
                    silu(1, i * 2 + 1)
                    read_y(0, i * 2, i * 16)

                pair_of(1, None)
                each_pair(act, pairs, 2, 6, lambda i: pair_of(i, i * 16 - 16))
                read_y(1, last_block(act), table(act, STORED_AT, 16, 16 * PAIRS))

            @block.vector
            def _(dve):
                def turn_x(q, g, i, first=False):
                    dve.wait_ge(gathered[q], (i + 1) * 16 * QUADS)
                    if not first:
                        dve.wait_ge(gu_done, g - 1)
                    nc.vector.transpose(
                        xT[q][:].rearrange("p k (q b) -> p q k b", q=QUADS),
                        xg[q][:].rearrange("p (q f k) -> p q k f", q=QUADS, k=KD)).then_inc(x_turned, 1)

                def hidden(q, g):
                    dve.wait_ge(silu_done, g + 1)
                    nc.vector.tensor_tensor(hid[q][:], gu[q][:, DE:2 * DE], sg[q][:], ALU.mult).then_inc(hid_ready, 1)

                def place_h(q, g):
                    dve.wait_ge(h_turned, g + 1)
                    nc.vector.tensor_copy(hT[q][:], hb[:]).then_inc(h_placed, 1)

                def read_y(q, g, n16):
                    dve.wait_ge(y_done, g + 1)
                    if n16 is not None:
                        dve.wait_ge(stored[q], n16)
                    nc.vector.tensor_copy(ys[q][:, 0:512], yb[0][:]).then_inc(y_v, 1)

                pairs = pair_count(dve)
                turn_x(0, 0, 0, True)
                turn_x(1, 1, 0, True)
                hidden(0, 0)
                place_h(0, 0)
                turn_x(0, 2, 1)
                hidden(1, 1)
                read_y(0, 0, None)
                place_h(1, 1)

                def pair_of(i, n16):
                    turn_x(1, i * 2 + 1, i)
                    hidden(0, i * 2)
                    read_y(1, i * 2 - 1, n16)
                    place_h(0, i * 2)
                    turn_x(0, i * 2 + 2, i + 1)
                    hidden(1, i * 2 + 1)
                    read_y(0, i * 2, i * 16)
                    place_h(1, i * 2 + 1)

                pair_of(1, None)
                each_pair(dve, pairs, 2, 6, lambda i: pair_of(i, i * 16 - 16))
                read_y(1, last_block(dve), table(dve, STORED_AT, 16, 16 * PAIRS))


def combine(tr, layer, f, tiles):
    nc, dr = tr.nc, tr.dram
    n_t = len(tiles)
    BUFS = 12
    seq = [(n + i, k) for n in range(0, n_t, 2) for k in range(TOPK) for i in range(2)]
    last = layer == DEPTH - 1
    kinds = [0, 1] if tiles[0] < CT else [0]
    with Phase(nc) as ph:
        got = [ph.sb(f"got{i}", [P, D]) for i in range(BUFS)]
        post = ph.sb("post", [P, len(kinds), D])
        sq = ph.sb("sq", [P, D])
        fs = [ph.sb(f"fs{i}", [P, D]) for i in range(2)]
        ss, rt, rs = ph.sb("ss", [P, n_t]), ph.sb("rt", [P, n_t]), ph.sb("rs", [P, n_t])
        loaded, fetched = ph.sem("loaded"), [ph.sem(f"fetched{i}") for i in range(BUFS)]
        added, squared, rooted = ph.sem("added"), ph.sem("squared"), ph.sem("rooted")
        h_sq, h_rt = ph.sb("h_sq", [P, D]), ph.sb("h_rt", [P, NT])
        h_squared, h_rooted = ph.sem("h_squared"), ph.sem("h_rooted")
        inverted, scaled, h_done, stored = ph.sem("inverted"), ph.sem("scaled"), ph.sem("h_done"), ph.sem("stored")
        with ph.block() as block:
            @block.sync
            def _(sp):
                y = tr.rows_y.rearrange("(t p k) n -> t p k n", p=P, k=TOPK)
                for j, (n, k) in enumerate(seq):
                    if j >= BUFS:
                        sp.wait_ge(added, j - BUFS + 1)
                    sp.dma_start(got[j % BUFS][:], y[tiles[n], :, k, :]).then_inc(fetched[j % BUFS], 16)

            @block.gpsimd
            def _(pool):
                for s in kinds:
                    pool.dma_start(post[:, s, :], mod_vector(tr, layer, 3, s)).then_inc(loaded, 16)
                for n, t in enumerate(tiles[:-2]):
                    pool.wait_ge(scaled, n + 1)
                    nc.gpsimd.tensor_tensor(tr.h[:, t, :], tr.h[:, t, :], fs[n % 2][:], ALU.add).then_inc(h_done, 1)
                    if last:
                        pool.wait_ge(h_done, n + 1)
                        pool.dma_start(tr.out[0, (t - CT) * P:(t - CT + 1) * P, :], tr.h[:, t, :]).then_inc(stored, 16)
                if last:
                    for n, t in list(enumerate(tiles))[-2:]:
                        pool.wait_ge(h_done, n + 1)
                        pool.dma_start(tr.out[0, (t - CT) * P:(t - CT + 1) * P, :], tr.h[:, t, :]).then_inc(stored, 16)
                    pool.wait_ge(stored, 16 * n_t)

            @block.scalar
            def _(act):
                for n, t in enumerate(tiles):
                    act.wait_ge(added, seq.index((n, TOPK - 1)) + 1)
                    if n:
                        act.wait_ge(squared, n)
                    nc.scalar.activation(sq[:], f[:, t, :], ACT.Square, accum_out=ss[:, n:n + 1]).then_inc(squared, 1)
                    act.wait_ge(squared, n + 1)
                    nc.scalar.activation(rt[:, n:n + 1], ss[:, n:n + 1], ACT.Sqrt, bias=tr.eps[:, 0:1],
                                         scale=1.0 / D).then_inc(rooted, 1)
                    if n % 2 and not last:
                        for i in (n - 1, n):
                            act.wait_ge(h_done, i + 1)
                            if i:
                                act.wait_ge(h_squared, i)
                            nc.scalar.activation(h_sq[:], tr.h[:, tiles[i], :], ACT.Square,
                                                 accum_out=tr.h_ss[:, tiles[i]:tiles[i] + 1]).then_inc(h_squared, 1)
                if not last:
                    act.wait_ge(h_squared, n_t)
                    nc.scalar.activation(h_rt[:], tr.h_ss[:], ACT.Sqrt, bias=tr.eps[:, 0:1], scale=1.0 / D) \
                        .then_inc(h_rooted, 1)

            @block.vector
            def _(dve):
                dve.wait_ge(loaded, 16 * len(kinds))

                def finish(n):
                    t = tiles[n]
                    dve.wait_ge(rooted, n + 1)
                    nc.vector.reciprocal(rs[:, n:n + 1], rt[:, n:n + 1]).then_inc(inverted, 1)
                    dve.wait_ge(inverted, n + 1)
                    if n >= 2:
                        dve.wait_ge(h_done, n - 1)
                    nc.vector.scalar_tensor_tensor(fs[n % 2][:], f[:, t, :], rs[:, n:n + 1],
                                                   post[:, 1 if t < CT else 0, :], ALU.mult, ALU.mult) \
                        .then_inc(scaled, 1)
                    if n >= n_t - 2:
                        dve.wait_ge(scaled, n + 1)
                        dve.wait_ge(h_done, n)
                        nc.vector.tensor_tensor(tr.h[:, t, :], tr.h[:, t, :], fs[n % 2][:], ALU.add).then_inc(h_done, 1)

                for j, (n, k) in enumerate(seq):
                    t = tiles[n]
                    dve.wait_ge(fetched[j % BUFS], 16 * (j // BUFS + 1))
                    if k:
                        dve.wait_ge(added, j - 1)
                    nc.vector.scalar_tensor_tensor(f[:, t, :], got[j % BUFS][:], tr.w8[:, n, k:k + 1],
                                                   f[:, t, :], ALU.mult, ALU.add).then_inc(added, 1)
                    if k == 2 and n >= 2:
                        finish(n - 2)
                finish(n_t - 2)
                finish(n_t - 1)
                if not last:
                    dve.wait_ge(h_rooted, 1)
                    nc.vector.reciprocal(tr.h_rs[:], h_rt[:])


def mix_and_route(tr, layer, cat, tiles, w, w_loaded):
    with tr.nc.sbuf_tensor(f"vT{layer}", [P, KD, T], F32) as vT:
        mix_out(tr, layer, cat, vT, tiles, w, w_loaded)
        route(tr, layer, vT, cat, tiles)


def experts_and_sum(tr, layer, f, tiles):
    experts(tr, layer)
    combine(tr, layer, f, tiles)


KR2 = MQR + MKR + 2 * MR


def load_w_in_o(eng, tr, w, loaded):
    w_dram = tr.dram["w_in_o"][0].rearrange("(p k) n -> p k n", k=KD)
    eng.dma_start(w[:, :, ODD_IN:KR2], w_dram[:, :, ODD_IN - MR:ODD_IN]).then_inc(loaded, 16)
    eng.dma_start(w[:, :, 0:ODD_IN], w_dram).then_inc(loaded, 16)


def load_w_uq(eng, tr, wn, wr, loaded):
    uq = tr.dram["w_uq"][0].rearrange("(p k) (h n) -> k p h n", k=MQR // P, h=MH)
    for k in range(MQR // P):
        eng.dma_start(wn[:, k], uq[k][:, :, 0:MN]).then_inc(loaded, 16)
        eng.dma_start(wr[:, k], uq[k][:, :, MN:MN + MR]).then_inc(loaded, 16)


def odd_project(tr, uT, cqT, ckvT, krT, w, w_loaded, load_ahead):
    nc, dr = tr.nc, tr.dram
    HALF = T // 2
    KQ, KK = MQR // P, MKR // P
    with Phase(nc) as ph:
        ph.adopt([w_loaded])
        gq, gk = ph.sb("gq", [P, KQ]), ph.sb("gk", [P, KK])
        sq = ph.sb("sq", [P, MQR])
        ss, rt, rs = ph.sb("ss", [P, NT, 2]), ph.sb("rt", [P, NT, 2]), ph.sb("rs", [P, NT, 2])
        row = [ph.sb(f"row{i}", [P, MQR + MKR]) for i in range(2)]
        qb = [ph.ps(f"qb{i}", [P, MQR]) for i in range(2)]
        kb = [ph.ps(f"kb{i}", [P, 512]) for i in range(2)]
        tq, tk = ph.ps("tq", [P, KQ, P]), ph.ps("tk", [P, KK, P])
        rb = [ph.ps(f"rb{i}", [P, 512]) for i in range(2)]
        loaded, rope_done, down_done = ph.sem("loaded"), ph.sem("rope_done"), ph.sem("down_done")
        squared, rooted, inverted = ph.sem("squared"), ph.sem("rooted"), ph.sem("inverted")
        rows_done, turned, placed = ph.sem("rows_done"), ph.sem("turned"), ph.sem("placed")
        with ph.block() as block:
            @block.sync
            def _(sp):
                sp.dma_start(gq[:], dr["mla_q_norm"][0].rearrange("(p k) -> p k", k=KQ)).then_inc(loaded, 16)
                sp.dma_start(gk[:], dr["mla_kv_norm"][0].rearrange("(p k) -> p k", k=KK)).then_inc(loaded, 16)
                load_ahead(sp)

            @block.tensor
            def _(pe):
                pe.wait_ge(w_loaded, 32)
                for hf in range(2):
                    for k in range(KD):
                        mm = nc.tensor.matmul(rb[hf][:, 0:HALF], w[:, k, MQR + MKR:KR2],
                                              uT[:, k, hf * HALF:(hf + 1) * HALF], start=(k == 0), stop=(k == KD - 1))
                    mm.then_inc(rope_done, 1)

                def down(t):
                    if t >= 2:
                        pe.wait_ge(rows_done, t - 1)
                    lhs = uT[:, :, t * P:(t + 1) * P]
                    if t >= CT:
                        for k in range(KD):
                            nc.tensor.matmul(qb[t % 2][:], lhs[:, k, :], w[:, k, 0:MQR],
                                             start=(k == 0), stop=(k == KD - 1))
                    for k in range(KD):
                        mm = nc.tensor.matmul(kb[t % 2][:, 0:MKR], lhs[:, k, :], w[:, k, MQR:MQR + MKR],
                                              start=(k == 0), stop=(k == KD - 1))
                    mm.then_inc(down_done, 1)

                def turn(t):
                    pe.wait_ge(rows_done, t + 1)
                    if t:
                        pe.wait_ge(placed, t)
                    if t >= CT:
                        for k in range(KQ):
                            nc.tensor.transpose(tq[:, k, :], row[t % 2][:, k:MQR:KQ], tr.ident[:])
                    for k in range(KK):
                        mm = nc.tensor.transpose(tk[:, k, :], row[t % 2][:, MQR + k:MQR + MKR:KK], tr.ident[:])
                    mm.then_inc(turned, 1)

                down(0)
                for t in range(NT):
                    if t + 1 < NT:
                        down(t + 1)
                    turn(t)

            @block.scalar
            def _(act):
                for hf in range(2):
                    act.wait_ge(rope_done, hf + 1)
                    nc.scalar.copy(krT[:, hf * HALF:(hf + 1) * HALF], rb[hf][:, 0:HALF])
                n = 0
                for t in range(NT):
                    act.wait_ge(down_done, t + 1)
                    for i, (src, width) in enumerate(((qb[t % 2][:], MQR), (kb[t % 2][:, 0:MKR], MKR))):
                        if i == 0 and t < CT:
                            continue
                        if n:
                            act.wait_ge(squared, n)
                        nc.scalar.activation(sq[:, 0:width], src, ACT.Square, accum_out=ss[:, t, i:i + 1]) \
                            .then_inc(squared, 1)
                        n += 1
                        act.wait_ge(squared, n)
                        nc.scalar.activation(rt[:, t, i:i + 1], ss[:, t, i:i + 1], ACT.Sqrt, bias=tr.eps[:, 0:1],
                                             scale=1.0 / width).then_inc(rooted, 1)

            @block.vector
            def _(dve):
                dve.wait_ge(loaded, 32)
                n = 0

                def place(t):
                    dve.wait_ge(turned, t + 1)
                    if t >= CT:
                        q = t - CT
                        nc.vector.tensor_tensor(cqT[:, :, q * P:(q + 1) * P], tq[:],
                                                gq[:].unsqueeze(2).to_broadcast([P, KQ, P]), ALU.mult)
                    nc.vector.tensor_tensor(ckvT[:, :, t * P:(t + 1) * P], tk[:],
                                            gk[:].unsqueeze(2).to_broadcast([P, KK, P]), ALU.mult) \
                        .then_inc(placed, 1)

                for t in range(NT):
                    first = 0 if t >= CT else 1
                    n += 2 - first
                    dve.wait_ge(rooted, n)
                    nc.vector.reciprocal(rs[:, t, first:2], rt[:, t, first:2]).then_inc(inverted, 1)
                    dve.wait_ge(inverted, t + 1)
                    if t >= 2:
                        dve.wait_ge(turned, t - 1)
                    if t >= CT:
                        nc.vector.tensor_scalar(row[t % 2][:, 0:MQR], qb[t % 2][:], rs[:, t, 0:1], None, ALU.mult)
                    nc.vector.tensor_scalar(row[t % 2][:, MQR:MQR + MKR], kb[t % 2][:, 0:MKR], rs[:, t, 1:2], None,
                                            ALU.mult).then_inc(rows_done, 1)
                    if t:
                        place(t - 1)
                place(NT - 1)


def latent_up(tr, cqT, ckvT, qnT, qrT, knT, v, wn, wr, q_loaded):
    nc, dr = tr.nc, tr.dram
    HALF = T // 2
    KQ, KK = MQR // P, MKR // P
    NB = 8
    jobs = [("qn", h, 0) for h in range(MH)] + [("qr", j, 0) for j in range(MH // 2)]
    jobs += [("kn", h, hf) for h in range(MH) for hf in range(2)] + [("v", t, hf) for t in range(NT) for hf in range(2)]
    engines = [("dve", "act")[n % 2] for n in range(len(jobs))]
    drains = Drains(engines)
    with Phase(nc) as ph:
        ph.adopt([q_loaded])
        wk = ph.sb("wk", [P, KK, MH, MN + MV])
        bank = [ph.ps(f"bank{i}", [P, 512]) for i in range(NB)]
        kv_loaded, product = ph.sem("kv_loaded"), ph.sem("product")
        read_dve, read_act = ph.sem("read_dve"), ph.sem("read_act")

        def target(kind, i, x):
            if kind == "qn":
                return qnT[:, i, :], NLAT
            if kind == "qr":
                return qrT[:, i, :], NLAT
            if kind == "kn":
                return knT[:, i, x * HALF:(x + 1) * HALF], HALF
            return v[:, i, x * 512:(x + 1) * 512], 512

        with ph.block() as block:
            @block.sync
            def _(sp):
                sp.dma_start(wk[:].rearrange("p k h n -> p k (h n)"),
                             dr["w_ukv"][0].rearrange("(p k) n -> p k n", k=KK)).then_inc(kv_loaded, 16)

            @block.tensor
            def _(pe):
                pe.wait_ge(q_loaded, 32 * KQ)
                for n, (kind, i, x) in enumerate(jobs):
                    if kind == "kn" and jobs[n - 1][0] != "kn":
                        pe.wait_ge(kv_loaded, 16)
                    if n >= NB:
                        e = engines[n - NB]
                        pe.wait_ge(read_dve if e == "dve" else read_act, drains.count(n - NB + 1, e))
                    o = bank[n % NB][:, 0:target(kind, i, x)[1]]
                    ks = KQ if kind in ("qn", "qr") else KK
                    for k in range(ks):
                        if kind == "qn":
                            lhs, rhs = wn[:, k, i, :], cqT[:, k, :]
                        elif kind == "qr":
                            lhs, rhs = wr[:, k, 2 * i:2 * i + 2, :].rearrange("p h n -> p (h n)"), cqT[:, k, :]
                        elif kind == "kn":
                            lhs, rhs = wk[:, k, i, 0:MN], ckvT[:, k, x * HALF:(x + 1) * HALF]
                        else:
                            lhs = ckvT[:, k, i * P:(i + 1) * P]
                            rhs = wk[:, k, 4 * x:4 * x + 4, MN:MN + MV]
                        mm = nc.tensor.matmul(o, lhs, rhs, start=(k == 0), stop=(k == ks - 1))
                    mm.then_inc(product, 1)

            @block.vector
            def _(dve):
                for n, job in enumerate(jobs):
                    if engines[n] == "dve":
                        dst, cnt = target(*job)
                        dve.wait_ge(product, n + 1)
                        nc.vector.tensor_copy(dst, bank[n % NB][:, 0:cnt]).then_inc(read_dve, 1)

            @block.scalar
            def _(act):
                for n, job in enumerate(jobs):
                    if engines[n] == "act":
                        dst, cnt = target(*job)
                        act.wait_ge(product, n + 1)
                        nc.scalar.copy(dst, bank[n % NB][:, 0:cnt]).then_inc(read_act, 1)


def latent_attention(tr, qnT, qrT, knT, krT, v, cat, load_ahead):
    nc = tr.nc
    QT = NLAT // P
    N = QT * MH
    with Phase(nc) as ph:
        p = [ph.sb(f"p{i}", [P, T]) for i in range(2)]
        pT = [ph.sb(f"pT{i}", [P, NT, P]) for i in range(2)]
        m, nm = ph.sb("m", [P, N]), ph.sb("nm", [P, N])
        total, rden = ph.sb("total", [P, N]), ph.sb("rden", [P, N])
        raw = [ph.ps(f"raw{i}", [P, 1024]) for i in range(2)]
        turn = [ph.ps(f"turn{i}", [P, 4, P]) for i in range(2)]
        op = [ph.ps(f"op{i}", [P, 4, MV]) for i in range(2)]
        scored, maxed, negated, probs = ph.sem("scored"), ph.sem("maxed"), ph.sem("negated"), ph.sem("probs_ready")
        turned, placed_v, placed_a = ph.sem("turned"), ph.sem("placed_v"), ph.sem("placed_a")
        attended, inverted, normed = ph.sem("attended"), ph.sem("inverted"), ph.sem("normed")
        with ph.block() as block:
            @block.sync
            def _(sp):
                load_ahead(sp)

            @block.tensor
            def _(pe):
                def scores(n):
                    qt, h = divmod(n, MH)
                    if n >= 2:
                        pe.wait_ge(probs, n - 1)
                    cols = slice(qt * P, (qt + 1) * P)
                    r = slice((h % 2) * MR, (h % 2 + 1) * MR)
                    for lo, hi in ((0, 512), (512, T)):
                        nc.tensor.matmul(raw[n % 2][:, lo:hi], qnT[:, h, cols], knT[:, h, lo:hi], start=True, stop=False)
                        mm = nc.tensor.matmul(raw[n % 2][:, lo:hi], qrT[r, h // 2, cols], krT[r, lo:hi],
                                              start=False, stop=True)
                    mm.then_inc(scored, 1)

                def turn_probs(n):
                    pe.wait_ge(probs, n + 1)
                    for half, bs in enumerate((range(0, 4), range(4, NT))):
                        if n:
                            pe.wait_ge(placed_a if half else placed_v, n)
                        for b in bs:
                            mm = nc.tensor.transpose(turn[half][:, b % 4, :], p[n % 2][:, b * P:(b + 1) * P],
                                                     tr.ident[:])
                        mm.then_inc(turned, 1)

                def values(n):
                    h = n % MH
                    g = n // 4
                    pe.wait_ge(placed_v, n + 1)
                    pe.wait_ge(placed_a, n + 1)
                    if n % 4 == 0 and g >= 2:
                        pe.wait_ge(normed, g - 1)
                    for b in range(NT):
                        mm = nc.tensor.matmul(op[g % 2][:, n % 4, :], pT[n % 2][:, b, :],
                                              v[:, b, h * MV:(h + 1) * MV], start=(b == 0), stop=(b == NT - 1))
                    mm.then_inc(attended, 1)

                scores(0)
                for n in range(N):
                    if n + 1 < N:
                        scores(n + 1)
                    turn_probs(n)
                    if n:
                        values(n - 1)
                values(N - 1)

            @block.vector
            def _(dve):
                def top(n):
                    dve.wait_ge(scored, n + 1)
                    nc.vector.reduce_max(m[:, n:n + 1], raw[n % 2][:, 0:T], AX).then_inc(maxed, 1)
                    dve.wait_ge(maxed, n + 1)
                    nc.vector.tensor_scalar(nm[:, n:n + 1], m[:, n:n + 1], -MSCALE, None, ALU.mult) \
                        .then_inc(negated, 1)

                def norm(g):
                    dve.wait_ge(probs, 4 * g + 4)
                    nc.vector.reciprocal(rden[:, 4 * g:4 * g + 4], total[:, 4 * g:4 * g + 4]).then_inc(inverted, 1)
                    dve.wait_ge(inverted, g + 1)
                    dve.wait_ge(attended, 4 * g + 4)
                    qt, q = divmod(g, 2)
                    nc.vector.tensor_tensor(
                        cat[:, CT + qt, q * 512:(q + 1) * 512].rearrange("p (h e) -> p h e", h=4), op[g % 2][:],
                        rden[:, 4 * g:4 * g + 4].unsqueeze(2).to_broadcast([P, 4, MV]), ALU.mult).then_inc(normed, 1)

                top(0)
                for n in range(N):
                    if n + 1 < N:
                        top(n + 1)
                    dve.wait_ge(turned, 2 * n + 1)
                    if n >= 2:
                        dve.wait_ge(attended, n - 1)
                    nc.vector.tensor_copy(pT[n % 2][:, 0:4, :], turn[0][:]).then_inc(placed_v, 1)
                    if n % 4 == 0 and n:
                        norm(n // 4 - 1)
                norm(N // 4 - 1)

            @block.scalar
            def _(act):
                def exp(n):
                    act.wait_ge(negated, n + 1)
                    if n >= 2:
                        act.wait_ge(turned, 2 * (n - 1))
                    nc.scalar.activation(p[n % 2][:], raw[n % 2][:, 0:T], ACT.Exp, bias=nm[:, n:n + 1], scale=MSCALE,
                                         accum_out=total[:, n:n + 1]).then_inc(probs, 1)

                exp(0)
                for n in range(N):
                    if n + 1 < N:
                        exp(n + 1)
                    act.wait_ge(turned, 2 * n + 2)
                    if n >= 2:
                        act.wait_ge(attended, n - 1)
                    nc.scalar.copy(pT[n % 2][:, 4:NT, :], turn[1][:, 0:NT - 4, :]).then_inc(placed_a, 1)


def odd_mixer(tr, layer):
    nc = tr.nc
    with ExitStack() as st:
        def sb(name, shape):
            return st.enter_context(nc.sbuf_tensor(name, shape, F32))

        cat = sb("cat_o", [P, NT, D])
        with ExitStack() as st:
            w = sb("w_o", [P, KD, D])
            w_down = w[:].rearrange("p k n -> p (k n)")[:, 0:KD * KR2].rearrange("p (k n) -> p k n", k=KD)
            down_loaded, uq_loaded, out_loaded = (nc.alloc_semaphore(f"w_{x}_loaded") for x in ("down", "uq", "out"))
            spare = cat[:].rearrange("p t n -> p (t n)")
            KQ = MQR // P
            wn = spare[:, 0:KQ * MH * MN].rearrange("p (k h n) -> p k h n", k=KQ, h=MH)
            wr = spare[:, KQ * MH * MN:KQ * MH * (MN + MR)].rearrange("p (k h n) -> p k h n", k=KQ, h=MH)
            with ExitStack() as st:
                qnT, qrT = sb("qnT", [P, MH, NLAT]), sb("qrT", [P, MH // 2, NLAT])
                knT, krT, v = sb("knT", [P, MH, T]), sb("krT", [P, T]), sb("v_o", [P, NT, MH * MV])
                with ExitStack() as st:
                    cqT, ckvT = sb("cqT", [P, MQR // P, NLAT]), sb("ckvT", [P, MKR // P, T])
                    with nc.sbuf_tensor("uT_o", [P, KD, T], F32) as uT:
                        norm_transpose(tr, layer, uT, lambda sp: load_w_in_o(sp, tr, w_down, down_loaded))
                        odd_project(tr, uT, cqT, ckvT, krT, w_down, down_loaded,
                                    lambda sp: load_w_uq(sp, tr, wn, wr, uq_loaded))
                    latent_up(tr, cqT, ckvT, qnT, qrT, knT, v, wn, wr, uq_loaded)
                rotate(tr, [qrT[:, i, :] for i in range(MH // 2)] + [krT[:, NCTX:T]])
                latent_attention(tr, qnT, qrT, knT, krT, v, cat, lambda sp: sp.dma_start(
                    w[:], tr.dram["w_out_o"][0].rearrange("(p k) n -> p k n", k=KD)).then_inc(out_loaded, 16))
            mix_and_route(tr, layer, cat, list(range(CT, NT)), w, out_loaded)
        experts_and_sum(tr, layer, cat, list(range(CT, NT)))


def build(nc, dram, out):
    tr = Trunk(nc, dram, out)
    with ExitStack() as st:
        def sb(name, shape, dt=F32):
            return st.enter_context(nc.sbuf_tensor(name, shape, dt))

        Phase.opened = 0
        tr.h = sb("h", [P, NT, D])
        tr.slot_pair = sb("slot_pair", [P, SLOTB], I32)
        tr.slot_row, tr.blocks = sb("slot_row", [P, QUADS, SLOTB], I32), sb("blocks", [1, TABLE], I32)
        tr.dest8, tr.w8 = sb("dest8", [P, NT, TOPK], I32), sb("w8", [P, NT, TOPK])
        tr.pre_scale, tr.pre_shift = sb("pre_scale", [P, DEPTH, KD, 2]), sb("pre_shift", [P, DEPTH, KD, 2])
        tr.silu_c = sb("silu_c", [P, KD, 2])
        tr.h_ss, tr.h_rs = sb("h_ss", [P, NT]), sb("h_rs", [P, NT])
        tr.ident, tr.ones, tr.eps = sb("ident", [P, P]), sb("ones", [P, P]), sb("eps", [P, 1])
        tr.mod_raw = nc.dram_tensor("mod_raw", [DEPTH, 2, 6 * D], F32)
        tr.mod_row = nc.dram_tensor("mod_row", [DEPTH, 4, 2, D], F32)
        tr.slot_name = [nc.dram_tensor(f"slot_name{i}", [SLOTB * P, 1], F32) for i in range(DEPTH)]
        tr.rows_x = nc.dram_tensor("rows_x", [T, D], F32)
        tr.rows_y = nc.dram_tensor("rows_y", [T * TOPK, D], F32)
        start(tr)
        for layer in range(DEPTH):
            if layer % 2 == 0:
                even_mixer(tr, layer)
            else:
                odd_mixer(tr, layer)


GRID_W, THETA = 64, 10000.0


def _constants():
    j, i = np.arange(P)[:, None], np.arange(P)[None, :]
    f32 = np.float32
    tok = np.arange(NLAT)
    axis = SHD // 2
    inv = f32(THETA) ** (-np.arange(0, axis, 2, dtype=f32) / f32(axis))
    ang = np.concatenate([(tok // GRID_W).astype(f32)[:, None] * inv, (tok % GRID_W).astype(f32)[:, None] * inv], 1)
    ang = np.tile(ang.T, (4, 1))
    half = SHD // 2
    swap = np.zeros((P, P), f32)
    for o in range(P):
        if o % SHD < half:
            swap[o + half, o] = -1.0
        else:
            swap[o - half, o] = 1.0
    ahead = np.where(j <= i, 0.0, NEG)
    behind = np.where(i >= j, 0.0, NEG)
    zero = np.zeros((P, P))
    band = np.stack([np.concatenate([zero, zero, np.where(i >= j, 0.0, NEG), zero, np.where(i <= j, 0.0, NEG)], 1),
                     np.concatenate([zero, zero, zero, np.where(i <= j, 0.0, NEG), zero], 1)], 1)
    return {
        "c_ident": np.eye(P, dtype=f32),
        "c_causal": np.stack([j <= i, j >= i], 1).astype(f32),
        "c_rope": np.stack([np.cos(ang), np.sin(ang)], 1).astype(f32),
        "c_swap": swap,
        "c_band": band.astype(f32),
        "c_before": (j < i).astype(f32),
        "c_row": np.arange(P)[:, None].astype(f32),
        "c_quad": (np.arange(P) // (P // QUADS))[:, None].astype(f32),
        "c_name": (np.arange(P)[:, None, None] * TOPK + P * TOPK * np.arange(NT)[None, :, None]
                   + np.arange(TOPK)[None, None, :]).astype(f32),
    }


_INS = ["x", "c", "ctx", "c_ctx", "w_mod", "b_mod", "g_mix_pre", "g_mix_post", "g_ffn_pre", "g_ffn_post",
        "w_in_e", "gla_wa2", "gla_ba", "gla_norm", "swa_sink", "w_out_e",
        "w_in_o", "mla_q_norm", "mla_kv_norm", "w_uq", "w_ukv", "w_out_o",
        "w_router", "b_router", "w_exp_gate", "w_exp_up", "w_exp_down", "w_sh_gate", "w_sh_up", "w_sh_down"]


def kernel(**inputs):
    import concourse.bacc as _bacc
    from concourse.bass_utils import run_bass_kernel_spmd as _run

    nc = _bacc.Bacc("TRN2", target_bir_lowering=False, num_devices=1)
    arrays, dram = {}, {}
    given = {n: np.ascontiguousarray(inputs[n]) for n in _INS}
    for name, a in {**given, **_constants()}.items():
        arrays[f"in_{name}"] = a
        dram[name] = nc.dram_tensor(f"in_{name}", a.shape, mybir.dt.from_np(a.dtype), kind="ExternalInput").ap()
    out = nc.dram_tensor("out_0", (1, NLAT, D), F32, kind="ExternalOutput").ap()
    build(nc, dram, out)
    r = _run(nc, [arrays], core_ids=[0])
    return r.results[0]["out_0"]
```
